# Optimizing a Trainium2 kernel written in Bass

```python
import math
import jax
import jax.numpy as jnp
from jax import lax
import numpy as np

D_MODEL = 1024
BATCH = 1
SEQ = 512
DEPTH = 2

GRID_W = 64
CTX_LEN = 256
N_MIXERS = 3
D_FF = 4 * D_MODEL
NORM_EPS = 1e-6

DN_K_HEADS = 8
DN_V_HEADS = 16
DN_HEAD_K = 128
DN_HEAD_V = 128
DN_GROUP = DN_V_HEADS // DN_K_HEADS
DN_K_DIM = DN_K_HEADS * DN_HEAD_K
DN_V_DIM = DN_V_HEADS * DN_HEAD_V
DN_QKV_DIM = 2 * DN_K_DIM + DN_V_DIM
DN_IN_DIM = DN_QKV_DIM + DN_V_DIM + 4 * DN_V_HEADS
SHORT_CONV = 5
DN_CHUNK = 64

GLA_HEADS = 4
GLA_K_DIM = D_MODEL // 2
GLA_V_DIM = D_MODEL
GLA_HEAD_K = GLA_K_DIM // GLA_HEADS
GLA_HEAD_V = GLA_V_DIM // GLA_HEADS
GLA_GATE_RANK = 16
GLA_GATE_NORMALIZER = 16.0
GLA_IN_DIM = 2 * GLA_K_DIM + 2 * GLA_V_DIM + 2 * GLA_GATE_RANK
GLA_CHUNK = 64

ATTN_Q_HEADS = 8
ATTN_KV_HEADS = 2
ATTN_HEAD_DIM = 128
ATTN_GROUP = ATTN_Q_HEADS // ATTN_KV_HEADS
ATTN_Q_DIM = ATTN_Q_HEADS * ATTN_HEAD_DIM
ATTN_KV_DIM = ATTN_KV_HEADS * ATTN_HEAD_DIM
ATTN_IN_DIM = ATTN_Q_DIM + 2 * ATTN_KV_DIM
Q_BLOCK = 128
ROPE_THETA = 10000.0


F32 = jnp.float32

def rms_norm(x, g):
    xf = x.astype(F32)
    y = xf * lax.rsqrt(jnp.mean(xf * xf, axis=-1, keepdims=True) + NORM_EPS)
    return (y * g.astype(F32)).astype(x.dtype)

def l2_normalize(x):
    xf = x.astype(F32)
    return xf * lax.rsqrt(jnp.sum(xf * xf, axis=-1, keepdims=True) + NORM_EPS)

def modulate(h, shift, scale):
    return h * (1.0 + scale) + shift

def squared_relu_ffn(h, w1, w2):
    return jnp.square(jax.nn.relu(h @ w1)) @ w2

def short_conv(u, w):
    n = u.shape[1]
    pad = SHORT_CONV // 2
    up = jnp.pad(u, ((0, 0), (pad, pad), (0, 0)))
    out = up[:, 0:n] * w[:, 0]
    for tap in range(1, SHORT_CONV):
        out = out + up[:, tap:tap + n] * w[:, tap]
    return out

def to_chunks(t, chunk):
    b, h, n = t.shape[:3]
    t = t.reshape((b, h, n // chunk, chunk) + t.shape[3:])
    return jnp.moveaxis(t, 2, 0)

def from_chunks(t):
    t = jnp.moveaxis(t, 0, 2)
    b, h, nc, chunk = t.shape[:4]
    return t.reshape((b, h, nc * chunk) + t.shape[4:])

def time_flip(t):
    return jnp.flip(t, axis=2)

def identity(t):
    return t

def axial_rope_tables(n_rows):
    row = jnp.repeat(jnp.arange(n_rows), GRID_W).astype(F32)
    col = jnp.tile(jnp.arange(GRID_W), n_rows).astype(F32)
    axis_dim = ATTN_HEAD_DIM // 2
    inv_freq = jnp.power(ROPE_THETA, -jnp.arange(0, axis_dim, 2, dtype=F32) / axis_dim)
    ang_row = row[:, None] * inv_freq
    ang_col = col[:, None] * inv_freq
    return jnp.cos(ang_row), jnp.sin(ang_row), jnp.cos(ang_col), jnp.sin(ang_col)

def rotate_pairs(x, cos, sin):
    x1, x2 = jnp.split(x, 2, axis=-1)
    cs, sn = cos[:, None, :], sin[:, None, :]
    return jnp.concatenate([x1 * cs - x2 * sn, x1 * sn + x2 * cs], axis=-1)

def apply_axial_rope(x, tables):
    cos_r, sin_r, cos_c, sin_c = tables
    xf = x.astype(F32)
    half = ATTN_HEAD_DIM // 2
    y = jnp.concatenate([rotate_pairs(xf[..., :half], cos_r, sin_r),
                         rotate_pairs(xf[..., half:], cos_c, sin_c)], axis=-1)
    return y.astype(x.dtype)

def gated_delta_rule(q, k, v, g, beta, state):
    c = DN_CHUNK
    tri = jnp.tril(jnp.ones((c, c), dtype=bool))
    strict = jnp.tril(jnp.ones((c, c), dtype=bool), -1)
    eye = jnp.eye(c, dtype=F32)

    def step(s, xs):
        qc, kc, vc, gc, bc = xs
        qc = jnp.repeat(qc, DN_GROUP, axis=1)
        kc = jnp.repeat(kc, DN_GROUP, axis=1)
        gcum = jnp.cumsum(gc, axis=-1)
        decay = jnp.exp(jnp.where(tri, gcum[..., :, None] - gcum[..., None, :], -jnp.inf))
        kk = jnp.einsum('bhid,bhjd->bhij', kc, kc)
        m = jnp.where(strict, bc[..., :, None] * kk * decay, 0.0)
        rhs = jnp.concatenate([vc * bc[..., None], kc * (bc * jnp.exp(gcum))[..., None]], axis=-1)
        sol = lax.linalg.triangular_solve(eye + m, rhs, left_side=True, lower=True, unit_diagonal=True)
        u, w = sol[..., :DN_HEAD_V], sol[..., DN_HEAD_V:]
        v_new = u - jnp.einsum('bhid,bhdv->bhiv', w, s)
        a_qk = jnp.einsum('bhid,bhjd->bhij', qc, kc) * decay
        o = (jnp.einsum('bhid,bhdv->bhiv', qc * jnp.exp(gcum)[..., None], s)
             + jnp.einsum('bhij,bhjv->bhiv', a_qk, v_new))
        tail = jnp.exp(gcum[..., -1:] - gcum)
        s = (s * jnp.exp(gcum[..., -1])[..., None, None]
             + jnp.einsum('bhjd,bhjv->bhdv', kc * tail[..., None], v_new))
        return s, o

    xs = (to_chunks(q, c), to_chunks(k, c), to_chunks(v, c), to_chunks(g, c), to_chunks(beta, c))
    state, o = lax.scan(step, state, xs)
    return from_chunks(o), state

def gla_rule(q, k, v, gk, state):
    c = GLA_CHUNK
    tri = jnp.tril(jnp.ones((c, c), dtype=bool))[:, :, None]

    def step(s, xs):
        qc, kc, vc, gc = xs
        bcum = jnp.cumsum(gc, axis=-2)
        rel = jnp.exp(jnp.where(tri, bcum[..., :, None, :] - bcum[..., None, :, :], -jnp.inf))
        a_qk = jnp.einsum('bhid,bhjd,bhijd->bhij', qc, kc, rel)
        o = (jnp.einsum('bhij,bhjv->bhiv', a_qk, vc)
             + jnp.einsum('bhid,bhdv->bhiv', qc * jnp.exp(bcum), s))
        last = bcum[..., -1:, :]
        s = (s * jnp.exp(last[..., 0, :])[..., None]
             + jnp.einsum('bhjd,bhjv->bhdv', kc * jnp.exp(last - bcum), vc))
        return s, o

    xs = (to_chunks(q, c), to_chunks(k, c), to_chunks(v, c), to_chunks(gk, c))
    state, o = lax.scan(step, state, xs)
    return from_chunks(o), state

def deltanet_mixer(hx, hc, w_in, conv_w, a_log, dt_bias, norm_g, w_out, with_ctx_out):
    def project(h):
        bsz, n, _ = h.shape
        p = h @ w_in
        qkv = jax.nn.silu(short_conv(p[..., :DN_QKV_DIM], conv_w))
        z = p[..., DN_QKV_DIM:DN_QKV_DIM + DN_V_DIM]
        ab = p[..., DN_QKV_DIM + DN_V_DIM:].astype(F32)
        q = l2_normalize(qkv[..., :DN_K_DIM].reshape(bsz, n, DN_K_HEADS, DN_HEAD_K)) * DN_HEAD_K ** -0.5
        k = l2_normalize(qkv[..., DN_K_DIM:2 * DN_K_DIM].reshape(bsz, n, DN_K_HEADS, DN_HEAD_K))
        v = qkv[..., 2 * DN_K_DIM:].reshape(bsz, n, DN_V_HEADS, DN_HEAD_V).astype(F32)
        a = ab[..., :2 * DN_V_HEADS].reshape(bsz, n, 2, DN_V_HEADS)
        b = ab[..., 2 * DN_V_HEADS:].reshape(bsz, n, 2, DN_V_HEADS)
        g = -jnp.exp(a_log.astype(F32)) * jax.nn.softplus(a + dt_bias.astype(F32))
        beta = jax.nn.sigmoid(b)
        return (jnp.swapaxes(q, 1, 2), jnp.swapaxes(k, 1, 2), jnp.swapaxes(v, 1, 2),
                jnp.moveaxis(g, 1, -1), jnp.moveaxis(beta, 1, -1), z)

    qx, kx, vx, gx, bx, zx = project(hx)
    qc, kc, vc, gc, bc, zc = project(hc)
    bsz = hx.shape[0]
    out_x, out_c = [], []
    for d in range(2):
        flip = time_flip if d == 1 else identity
        state0 = jnp.zeros((bsz, DN_V_HEADS, DN_HEAD_K, DN_HEAD_V), F32)
        oc, state_c = gated_delta_rule(flip(qc), flip(kc), flip(vc), flip(gc[:, d]), flip(bc[:, d]), state0)
        ox, _ = gated_delta_rule(flip(qx), flip(kx), flip(vx), flip(gx[:, d]), flip(bx[:, d]), state_c)
        out_x.append(flip(ox))
        out_c.append(flip(oc))

    def readout(o, z):
        bsz_, n = z.shape[:2]
        o = rms_norm(jnp.swapaxes(o, 1, 2), norm_g)
        o = o * jax.nn.silu(z.reshape(bsz_, n, DN_V_HEADS, DN_HEAD_V).astype(F32))
        return o.reshape(bsz_, n, DN_V_DIM).astype(z.dtype) @ w_out

    yx = readout(out_x[0] + out_x[1], zx)
    yc = readout(out_c[0] + out_c[1], zc) if with_ctx_out else None
    return yx, yc

def gla_mixer(hx, hc, w_in, gate_w2, gate_b2, norm_g, w_out, with_ctx_out):
    def project(h):
        bsz, n, _ = h.shape
        p = h @ w_in
        q = p[..., :GLA_K_DIM].reshape(bsz, n, GLA_HEADS, GLA_HEAD_K).astype(F32) * GLA_HEAD_K ** -0.5
        k = p[..., GLA_K_DIM:2 * GLA_K_DIM].reshape(bsz, n, GLA_HEADS, GLA_HEAD_K).astype(F32)
        v = p[..., 2 * GLA_K_DIM:2 * GLA_K_DIM + GLA_V_DIM].reshape(bsz, n, GLA_HEADS, GLA_HEAD_V).astype(F32)
        gate = p[..., 2 * GLA_K_DIM + GLA_V_DIM:2 * GLA_K_DIM + 2 * GLA_V_DIM]
        low = p[..., 2 * GLA_K_DIM + 2 * GLA_V_DIM:].reshape(bsz, n, 2, GLA_GATE_RANK)
        logits = jnp.einsum('btdr,drk->btdk', low, gate_w2) + gate_b2
        gk = jax.nn.log_sigmoid(logits.astype(F32)) / GLA_GATE_NORMALIZER
        gk = gk.reshape(bsz, n, 2, GLA_HEADS, GLA_HEAD_K).transpose(0, 2, 3, 1, 4)
        return jnp.swapaxes(q, 1, 2), jnp.swapaxes(k, 1, 2), jnp.swapaxes(v, 1, 2), gk, gate

    qx, kx, vx, gx, zx = project(hx)
    qc, kc, vc, gc, zc = project(hc)
    bsz = hx.shape[0]
    out_x, out_c = [], []
    for d in range(2):
        flip = time_flip if d == 1 else identity
        state0 = jnp.zeros((bsz, GLA_HEADS, GLA_HEAD_K, GLA_HEAD_V), F32)
        oc, state_c = gla_rule(flip(qc), flip(kc), flip(vc), flip(gc[:, d]), state0)
        ox, _ = gla_rule(flip(qx), flip(kx), flip(vx), flip(gx[:, d]), state_c)
        out_x.append(flip(ox))
        out_c.append(flip(oc))

    def readout(o, z):
        bsz_, n = z.shape[:2]
        o = rms_norm(jnp.swapaxes(o, 1, 2), norm_g)
        o = o * jax.nn.silu(z.reshape(bsz_, n, GLA_HEADS, GLA_HEAD_V).astype(F32))
        return o.reshape(bsz_, n, GLA_V_DIM).astype(z.dtype) @ w_out

    yx = readout(out_x[0] + out_x[1], zx)
    yc = readout(out_c[0] + out_c[1], zc) if with_ctx_out else None
    return yx, yc

def attention_mixer(hx, hc, w_in, q_norm_g, k_norm_g, w_out, rope, with_ctx_out):
    def project(h):
        bsz, n, _ = h.shape
        p = h @ w_in
        q = p[..., :ATTN_Q_DIM].reshape(bsz, n, ATTN_Q_HEADS, ATTN_HEAD_DIM)
        k = p[..., ATTN_Q_DIM:ATTN_Q_DIM + ATTN_KV_DIM].reshape(bsz, n, ATTN_KV_HEADS, ATTN_HEAD_DIM)
        v = p[..., ATTN_Q_DIM + ATTN_KV_DIM:].reshape(bsz, n, ATTN_KV_HEADS, ATTN_HEAD_DIM)
        return rms_norm(q, q_norm_g), rms_norm(k, k_norm_g), v

    qx, kx, vx = project(hx)
    qc, kc, vc = project(hc)
    qx = apply_axial_rope(qx, rope)
    kx = apply_axial_rope(kx, rope)
    bsz, n = hx.shape[:2]
    scale = ATTN_HEAD_DIM ** -0.5

    def attend(q_blk, keys, values):
        s = jnp.einsum('bkgqd,bksd->bkgqs', q_blk, keys).astype(F32) * scale
        p = jax.nn.softmax(s, axis=-1).astype(values.dtype)
        return jnp.einsum('bkgqs,bksd->bkgqd', p, values)

    k_all = jnp.concatenate([kx, kc], axis=1).transpose(0, 2, 1, 3)
    v_all = jnp.concatenate([vx, vc], axis=1).transpose(0, 2, 1, 3)
    n_blk = n // Q_BLOCK
    q_blocks = qx.reshape(bsz, n_blk, Q_BLOCK, ATTN_KV_HEADS, ATTN_GROUP, ATTN_HEAD_DIM).transpose(1, 0, 3, 4, 2, 5)
    o = lax.map(lambda qb: attend(qb, k_all, v_all), q_blocks)
    yx = o.transpose(1, 0, 4, 2, 3, 5).reshape(bsz, n, ATTN_Q_DIM) @ w_out
    yc = None
    if with_ctx_out:
        lc = hc.shape[1]
        q_ctx = qc.reshape(bsz, lc, ATTN_KV_HEADS, ATTN_GROUP, ATTN_HEAD_DIM).transpose(0, 2, 3, 1, 4)
        oc = attend(q_ctx, kc.transpose(0, 2, 1, 3), vc.transpose(0, 2, 1, 3))
        yc = oc.transpose(0, 3, 1, 2, 4).reshape(bsz, lc, ATTN_Q_DIM) @ w_out
    return yx, yc

def first_inputs(seed: int = 0) -> dict:
    key = jax.random.key(seed)
    ks = jax.random.split(key, 32)
    n_a = len(range(0, DEPTH, N_MIXERS))
    n_b = len(range(1, DEPTH, N_MIXERS))
    n_c = len(range(2, DEPTH, N_MIXERS))

    def normal(k, shape, scale):
        return jax.random.normal(k, shape, F32) * scale

    def gain(k, shape):
        return 1.0 + normal(k, shape, 0.02)

    dt = jnp.exp(jax.random.uniform(ks[12], (n_a, 2, DN_V_HEADS), F32, math.log(1e-3), math.log(1e-1)))
    return {
        'x': normal(ks[0], (BATCH, SEQ, D_MODEL), 1.0),
        'c': normal(ks[1], (BATCH, D_MODEL), 1.0),
        'ctx': normal(ks[2], (BATCH, CTX_LEN, D_MODEL), 1.0),
        'c_ctx': normal(ks[3], (D_MODEL,), 1.0),
        'ada_w': normal(ks[4], (DEPTH, D_MODEL, 6 * D_MODEL), 0.5 * D_MODEL ** -0.5),
        'ada_b': normal(ks[5], (DEPTH, 6 * D_MODEL), 0.01),
        'norm_mix_g': gain(ks[6], (DEPTH, D_MODEL)),
        'norm_ffn_g': gain(ks[7], (DEPTH, D_MODEL)),
        'ffn_w1': normal(ks[8], (DEPTH, D_MODEL, D_FF), D_MODEL ** -0.5),
        'ffn_w2': normal(ks[9], (DEPTH, D_FF, D_MODEL), D_FF ** -0.5),
        'dn_w_in': normal(ks[10], (n_a, D_MODEL, DN_IN_DIM), D_MODEL ** -0.5),
        'dn_conv_w': normal(ks[11], (n_a, DN_QKV_DIM, SHORT_CONV), SHORT_CONV ** -0.5),
        'dn_a_log': jnp.log(jax.random.uniform(ks[13], (n_a, 2, DN_V_HEADS), F32, 1.0, 16.0)),
        'dn_dt_bias': dt + jnp.log(-jnp.expm1(-dt)),
        'dn_norm_g': gain(ks[14], (n_a, DN_HEAD_V)),
        'dn_w_out': normal(ks[15], (n_a, DN_V_DIM, D_MODEL), DN_V_DIM ** -0.5),
        'gla_w_in': normal(ks[16], (n_b, D_MODEL, GLA_IN_DIM), D_MODEL ** -0.5),
        'gla_gate_w2': normal(ks[17], (n_b, 2, GLA_GATE_RANK, GLA_K_DIM), GLA_GATE_RANK ** -0.5),
        'gla_gate_b2': normal(ks[18], (n_b, 2, GLA_K_DIM), 0.1),
        'gla_norm_g': gain(ks[19], (n_b, GLA_HEAD_V)),
        'gla_w_out': normal(ks[20], (n_b, GLA_V_DIM, D_MODEL), GLA_V_DIM ** -0.5),
        'attn_w_in': normal(ks[21], (n_c, D_MODEL, ATTN_IN_DIM), D_MODEL ** -0.5),
        'attn_q_norm_g': gain(ks[22], (n_c, ATTN_HEAD_DIM)),
        'attn_k_norm_g': gain(ks[23], (n_c, ATTN_HEAD_DIM)),
        'attn_w_out': normal(ks[24], (n_c, ATTN_Q_DIM, D_MODEL), ATTN_Q_DIM ** -0.5),
    }

def first_block(x, c, ctx, c_ctx, ada_w, ada_b, norm_mix_g, norm_ffn_g, ffn_w1, ffn_w2,
              dn_w_in, dn_conv_w, dn_a_log, dn_dt_bias, dn_norm_g, dn_w_out,
              gla_w_in, gla_gate_w2, gla_gate_b2, gla_norm_g, gla_w_out,
              attn_w_in, attn_q_norm_g, attn_k_norm_g, attn_w_out):
    n_tok = x.shape[1]
    ROWS = n_tok // GRID_W
    rope = axial_rope_tables(ROWS)
    for i in range(DEPTH):
        with_ctx_out = i < DEPTH - 1
        mix, slot = i % N_MIXERS, i // N_MIXERS
        mod_x = jnp.split((jax.nn.silu(c) @ ada_w[i] + ada_b[i])[:, None, :], 6, axis=-1)
        mod_c = jnp.split(jax.nn.silu(c_ctx) @ ada_w[i] + ada_b[i], 6, axis=-1)
        hx = modulate(rms_norm(x, norm_mix_g[i]), mod_x[0], mod_x[1])
        hc = modulate(rms_norm(ctx, norm_mix_g[i]), mod_c[0], mod_c[1])
        if mix == 0:
            yx, yc = deltanet_mixer(hx, hc, dn_w_in[slot], dn_conv_w[slot], dn_a_log[slot], dn_dt_bias[slot],
                                    dn_norm_g[slot], dn_w_out[slot], with_ctx_out)
        elif mix == 1:
            yx, yc = gla_mixer(hx, hc, gla_w_in[slot], gla_gate_w2[slot], gla_gate_b2[slot],
                               gla_norm_g[slot], gla_w_out[slot], with_ctx_out)
        else:
            yx, yc = attention_mixer(hx, hc, attn_w_in[slot], attn_q_norm_g[slot], attn_k_norm_g[slot],
                                     attn_w_out[slot], rope, with_ctx_out)
        x = x + mod_x[2] * yx
        hx = modulate(rms_norm(x, norm_ffn_g[i]), mod_x[3], mod_x[4])
        x = x + mod_x[5] * squared_relu_ffn(hx, ffn_w1[i], ffn_w2[i])
        if with_ctx_out:
            ctx = ctx + mod_c[2] * yc
            hc = modulate(rms_norm(ctx, norm_ffn_g[i]), mod_c[3], mod_c[4])
            ctx = ctx + mod_c[5] * squared_relu_ffn(hc, ffn_w1[i], ffn_w2[i])
    return x


D_FF_2 = 4 * D_MODEL
ROPE_BASE = 10000.0

A_HEADS = 8
A_DQK = D_MODEL // (2 * A_HEADS)
A_DV = D_MODEL // A_HEADS
A_CHUNK = 128
A_IN = 2 * A_HEADS * A_DQK + A_HEADS * A_DV + D_MODEL + 4 * A_HEADS

SWA_HEADS = 16
SWA_KV_HEADS = 4
SWA_DH = D_MODEL // SWA_HEADS
SWA_GROUP = SWA_HEADS // SWA_KV_HEADS
WINDOW = 128
SWA_BLOCK = WINDOW
SWA_IN = (SWA_HEADS + 2 * SWA_KV_HEADS) * SWA_DH

DIFF_HEADS = 8
DIFF_DH = D_MODEL // (2 * DIFF_HEADS)
DIFF_DV = 2 * DIFF_DH
DIFF_BLOCK = 128
DIFF_IN = 4 * DIFF_HEADS * DIFF_DH + DIFF_HEADS * DIFF_DV

N_MLSTM = (DEPTH + N_MIXERS - 1) // N_MIXERS
N_SWA = (DEPTH + N_MIXERS - 2) // N_MIXERS
N_DIFF = (DEPTH + N_MIXERS - 3) // N_MIXERS


F32_2 = jnp.float32

def _rms_norm(x, g):
    xf = x.astype(F32_2)
    y = xf * lax.rsqrt(jnp.mean(xf * xf, axis=-1, keepdims=True) + NORM_EPS)
    return (y * g.astype(F32_2)).astype(x.dtype)

def _modulate(x, shift, scale):
    return x * (1.0 + scale) + shift

def _sq_relu_mlp(u, w1, w2):
    return jnp.square(jax.nn.relu(u @ w1)) @ w2

def _axial_rope_tables(n_tok, head_dim):
    rows = n_tok // GRID_W
    row = jnp.repeat(jnp.arange(rows, dtype=jnp.int32), GRID_W).astype(F32_2)
    col = jnp.tile(jnp.arange(GRID_W, dtype=jnp.int32), rows).astype(F32_2)
    quarter = head_dim // 4
    inv = ROPE_BASE ** (-jnp.arange(quarter, dtype=F32_2) / quarter)
    ang = jnp.concatenate([row[:, None] * inv, col[:, None] * inv], axis=-1)
    return jnp.cos(ang), jnp.sin(ang)

def _apply_rope(x, cos, sin):
    half = x.shape[-1] // 2
    x1, x2 = x[..., :half], x[..., half:]
    cs = cos[:, None, :].astype(x.dtype)
    sn = sin[:, None, :].astype(x.dtype)
    return jnp.concatenate([x1 * cs - x2 * sn, x1 * sn + x2 * cs], axis=-1)

def _to_chunks(t):
    bsz, n, h = t.shape[:3]
    t = t.reshape((bsz, n // A_CHUNK, A_CHUNK, h) + t.shape[3:])
    return jnp.moveaxis(t, 3, 1)

def _from_chunks(t):
    t = jnp.moveaxis(t, 1, 3)
    return t.reshape((t.shape[0], t.shape[1] * t.shape[2]) + t.shape[3:])

def _mlstm_direction(q, k, v, log_i, log_f, state, need_out):
    k_c, v_c = _to_chunks(k), _to_chunks(v)
    li, lf = _to_chunks(log_i), _to_chunks(log_f)
    b = jnp.cumsum(lf, axis=-1)
    b_last = b[..., -1]
    a = b_last[..., None] - b + li
    g = jnp.max(a, axis=-1)
    w = jnp.exp(a - g[..., None])
    kv = jnp.einsum("bhcs,bhcsd,bhcse->bhcde", w, k_c, v_c)
    kn = jnp.einsum("bhcs,bhcsd->bhcd", w, k_c)

    def step(carry, xs):
        c_st, n_st, m_st = carry
        bl, gj, kvj, knj = xs
        m_new = jnp.maximum(bl + m_st, gj)
        decay = jnp.exp(bl + m_st - m_new)
        inject = jnp.exp(gj - m_new)
        c_new = decay[..., None, None] * c_st + inject[..., None, None] * kvj
        n_new = decay[..., None] * n_st + inject[..., None] * knj
        return (c_new, n_new, m_new), (c_st, n_st, m_st)

    xs = (jnp.moveaxis(b_last, 2, 0), jnp.moveaxis(g, 2, 0), jnp.moveaxis(kv, 2, 0), jnp.moveaxis(kn, 2, 0))
    final, starts = lax.scan(step, state, xs)
    if not need_out:
        return None, final
    c0 = jnp.moveaxis(starts[0], 0, 2)
    n0 = jnp.moveaxis(starts[1], 0, 2)
    m0 = jnp.moveaxis(starts[2], 0, 2)
    q_c = _to_chunks(q)
    L = q_c.shape[-2]
    d = b[..., :, None] - b[..., None, :] + li[..., None, :]
    d = jnp.where(jnp.tril(jnp.ones((L, L), dtype=bool)), d, -jnp.inf)
    inter = b + m0[..., None]
    m_t = jnp.maximum(jnp.max(d, axis=-1), inter)
    wq = jnp.exp(d - m_t[..., None]) * jnp.einsum("bhctd,bhcsd->bhcts", q_c, k_c)
    carry_w = jnp.exp(inter - m_t)
    num = jnp.einsum("bhcts,bhcse->bhcte", wq, v_c) + carry_w[..., None] * jnp.einsum("bhctd,bhcde->bhcte", q_c, c0)
    den = jnp.sum(wq, axis=-1) + carry_w * jnp.einsum("bhctd,bhcd->bhct", q_c, n0)
    h = num / jnp.maximum(jnp.abs(den), jnp.exp(-m_t))[..., None]
    return _from_chunks(h), final

def _mlstm_mixer(u_ctx, u_lat, w_in, gate_b, head_norm, w_out, need_ctx):
    qk = A_HEADS * A_DQK
    vd = A_HEADS * A_DV
    splits = [qk, 2 * qk, 2 * qk + vd, 2 * qk + vd + D_MODEL]

    def project(u):
        bsz, n = u.shape[:2]
        q, k, v, o, gates = jnp.split(u @ w_in, splits, axis=-1)
        q = q.astype(F32_2).reshape(bsz, n, A_HEADS, A_DQK)
        k = k.astype(F32_2).reshape(bsz, n, A_HEADS, A_DQK) * (A_DQK ** -0.5)
        v = v.astype(F32_2).reshape(bsz, n, A_HEADS, A_DV)
        gates = gates.astype(F32_2).reshape(bsz, n, 4, A_HEADS) + gate_b.astype(F32_2)
        fwd = (gates[:, :, 0], jax.nn.log_sigmoid(gates[:, :, 1]))
        bwd = (gates[:, :, 2], jax.nn.log_sigmoid(gates[:, :, 3]))
        return q, k, v, o, fwd, bwd

    def flip(t):
        return jnp.flip(t, axis=1)

    cq, ck, cv, co, cf, cb = project(u_ctx)
    lq, lk, lv, lo, lf, lb = project(u_lat)
    bsz = u_lat.shape[0]
    zero = (jnp.zeros((bsz, A_HEADS, A_DQK, A_DV), F32_2), jnp.zeros((bsz, A_HEADS, A_DQK), F32_2),
            jnp.zeros((bsz, A_HEADS), F32_2))
    hcf, st_f = _mlstm_direction(cq, ck, cv, cf[0], cf[1], zero, need_ctx)
    hcb, st_b = _mlstm_direction(flip(cq), flip(ck), flip(cv), flip(cb[0]), flip(cb[1]), zero, need_ctx)
    hlf, _ = _mlstm_direction(lq, lk, lv, lf[0], lf[1], st_f, True)
    hlb, _ = _mlstm_direction(flip(lq), flip(lk), flip(lv), flip(lb[0]), flip(lb[1]), st_b, True)

    def finish(hf, hb, o):
        hs = hf + flip(hb)
        hn = hs * lax.rsqrt(jnp.mean(hs * hs, axis=-1, keepdims=True) + NORM_EPS)
        hn = hn * head_norm.astype(F32_2).reshape(A_HEADS, A_DV)
        bsz_, n = hs.shape[:2]
        return (hn.reshape(bsz_, n, vd).astype(o.dtype) * jax.nn.sigmoid(o)) @ w_out

    y_lat = finish(hlf, hlb, lo)
    y_ctx = finish(hcf, hcb, co) if need_ctx else None
    return y_lat, y_ctx

def _swa_mixer(u_ctx, u_lat, w_in, sink, w_out, cos, sin, need_ctx):
    scale = SWA_DH ** -0.5
    sink_g = sink.astype(F32_2).reshape(SWA_KV_HEADS, SWA_GROUP)[:, :, None]

    def project(u):
        bsz, n = u.shape[:2]
        q, k, v = jnp.split(u @ w_in, [SWA_HEADS * SWA_DH, (SWA_HEADS + SWA_KV_HEADS) * SWA_DH], axis=-1)
        return (q.reshape(bsz, n, SWA_HEADS, SWA_DH), k.reshape(bsz, n, SWA_KV_HEADS, SWA_DH),
                v.reshape(bsz, n, SWA_KV_HEADS, SWA_DH))

    cq, ck, cv = project(u_ctx)
    lq, lk, lv = project(u_lat)
    lq = _apply_rope(lq, cos, sin)
    lk = _apply_rope(lk, cos, sin)
    bsz, n_tok = u_lat.shape[:2]
    nb = n_tok // SWA_BLOCK
    kp = jnp.pad(lk, ((0, 0), (SWA_BLOCK, SWA_BLOCK), (0, 0), (0, 0)))
    vp = jnp.pad(lv, ((0, 0), (SWA_BLOCK, SWA_BLOCK), (0, 0), (0, 0)))
    q_blocks = jnp.moveaxis(lq.reshape(bsz, nb, SWA_BLOCK, SWA_KV_HEADS, SWA_GROUP, SWA_DH), 1, 0)
    q_idx = jnp.arange(SWA_BLOCK)[:, None]
    k_idx = jnp.arange(3 * SWA_BLOCK)[None, :]
    rel = k_idx - SWA_BLOCK - q_idx

    def block(args):
        j, qb = args
        kb = lax.dynamic_slice_in_dim(kp, j * SWA_BLOCK, 3 * SWA_BLOCK, axis=1)
        vb = lax.dynamic_slice_in_dim(vp, j * SWA_BLOCK, 3 * SWA_BLOCK, axis=1)
        kpos = j * SWA_BLOCK - SWA_BLOCK + k_idx
        valid = (jnp.abs(rel) <= WINDOW) & (kpos >= 0) & (kpos < n_tok)
        s_lat = jnp.einsum("bqhgd,bkhd->bhgqk", qb, kb).astype(F32_2) * scale
        s_lat = jnp.where(valid, s_lat, -jnp.inf)
        s_ctx = jnp.einsum("bqhgd,bchd->bhgqc", qb, ck).astype(F32_2) * scale
        m = jnp.maximum(jnp.maximum(jnp.max(s_lat, -1), jnp.max(s_ctx, -1)), sink_g)
        p_lat = jnp.exp(s_lat - m[..., None])
        p_ctx = jnp.exp(s_ctx - m[..., None])
        den = jnp.sum(p_lat, -1) + jnp.sum(p_ctx, -1) + jnp.exp(sink_g - m)
        o = jnp.einsum("bhgqk,bkhd->bqhgd", p_lat, vb) + jnp.einsum("bhgqc,bchd->bqhgd", p_ctx, cv)
        return o / jnp.moveaxis(den, 3, 1)[..., None]

    o_lat = lax.map(block, (jnp.arange(nb), q_blocks))
    o_lat = jnp.moveaxis(o_lat, 0, 1).reshape(bsz, n_tok, SWA_HEADS * SWA_DH)
    y_lat = o_lat.astype(u_lat.dtype) @ w_out
    if not need_ctx:
        return y_lat, None
    n_ctx = u_ctx.shape[1]
    cqg = cq.reshape(bsz, n_ctx, SWA_KV_HEADS, SWA_GROUP, SWA_DH)
    s = jnp.einsum("bqhgd,bchd->bhgqc", cqg, ck).astype(F32_2) * scale
    m = jnp.maximum(jnp.max(s, -1), sink_g)
    p = jnp.exp(s - m[..., None])
    den = jnp.sum(p, -1) + jnp.exp(sink_g - m)
    o_ctx = jnp.einsum("bhgqc,bchd->bqhgd", p, cv) / jnp.moveaxis(den, 3, 1)[..., None]
    y_ctx = o_ctx.reshape(bsz, n_ctx, SWA_HEADS * SWA_DH).astype(u_ctx.dtype) @ w_out
    return y_lat, y_ctx

def _diff_mixer(u_ctx, u_lat, w_in, lam_q1, lam_k1, lam_q2, lam_k2, head_norm, w_out, cos, sin,
                layer_idx, need_ctx):
    scale = DIFF_DH ** -0.5
    lam_init = 0.8 - 0.6 * math.exp(-0.3 * layer_idx)
    lam = (jnp.exp(jnp.sum(lam_q1.astype(F32_2) * lam_k1.astype(F32_2)))
           - jnp.exp(jnp.sum(lam_q2.astype(F32_2) * lam_k2.astype(F32_2))) + lam_init)
    qk = 2 * DIFF_HEADS * DIFF_DH

    def project(u, rope):
        bsz, n = u.shape[:2]
        q, k, v = jnp.split(u @ w_in, [qk, 2 * qk], axis=-1)
        q = q.reshape(bsz, n, 2 * DIFF_HEADS, DIFF_DH)
        k = k.reshape(bsz, n, 2 * DIFF_HEADS, DIFF_DH)
        if rope:
            q = _apply_rope(q, cos, sin)
            k = _apply_rope(k, cos, sin)
        return (q.reshape(bsz, n, DIFF_HEADS, 2, DIFF_DH), k.reshape(bsz, n, DIFF_HEADS, 2, DIFF_DH),
                v.reshape(bsz, n, DIFF_HEADS, DIFF_DV))

    def finish(o, dtype):
        od = o[:, :, :, 0] - lam * o[:, :, :, 1]
        od = od * lax.rsqrt(jnp.mean(od * od, axis=-1, keepdims=True) + NORM_EPS)
        od = od * head_norm.astype(F32_2).reshape(DIFF_HEADS, DIFF_DV) * (1.0 - lam_init)
        bsz, n = od.shape[:2]
        return od.reshape(bsz, n, DIFF_HEADS * DIFF_DV).astype(dtype) @ w_out

    cq, ck, cv = project(u_ctx, False)
    lq, lk, lv = project(u_lat, True)
    bsz, n_tok = u_lat.shape[:2]
    nb = n_tok // DIFF_BLOCK
    q_blocks = jnp.moveaxis(lq.reshape(bsz, nb, DIFF_BLOCK, DIFF_HEADS, 2, DIFF_DH), 1, 0)

    def block(qb):
        s_lat = jnp.einsum("bqhmd,bkhmd->bhmqk", qb, lk).astype(F32_2) * scale
        s_ctx = jnp.einsum("bqhmd,bchmd->bhmqc", qb, ck).astype(F32_2) * scale
        mx = jnp.maximum(jnp.max(s_lat, -1), jnp.max(s_ctx, -1))[..., None]
        p_lat = jnp.exp(s_lat - mx)
        p_ctx = jnp.exp(s_ctx - mx)
        den = jnp.sum(p_lat, -1) + jnp.sum(p_ctx, -1)
        o = jnp.einsum("bhmqk,bkhe->bqhme", p_lat, lv) + jnp.einsum("bhmqc,bche->bqhme", p_ctx, cv)
        return o / jnp.moveaxis(den, 3, 1)[..., None]

    o_lat = lax.map(block, q_blocks)
    o_lat = jnp.moveaxis(o_lat, 0, 1).reshape(bsz, n_tok, DIFF_HEADS, 2, DIFF_DV)
    y_lat = finish(o_lat, u_lat.dtype)
    if not need_ctx:
        return y_lat, None
    s = jnp.einsum("bqhmd,bkhmd->bhmqk", cq, ck).astype(F32_2) * scale
    a = jax.nn.softmax(s, axis=-1)
    o_ctx = jnp.einsum("bhmqk,bkhe->bqhme", a, cv)
    return y_lat, finish(o_ctx, u_ctx.dtype)

def second_inputs(seed: int = 0) -> dict:
    key = jax.random.key(seed)
    ks = jax.random.split(key, 25)
    D = D_MODEL

    def nrm(k, shape, scale):
        return jax.random.normal(k, shape, F32_2) * scale

    forget_bias = jnp.linspace(3.0, 6.0, A_HEADS, dtype=F32_2)
    zeros_h = jnp.zeros((A_HEADS,), F32_2)
    gate_base = jnp.stack([zeros_h, forget_bias, zeros_h, forget_bias])
    return {
        "x": nrm(ks[0], (BATCH, SEQ, D), 1.0),
        "c": nrm(ks[1], (BATCH, D), 1.0),
        "ctx": nrm(ks[2], (BATCH, CTX_LEN, D), 1.0),
        "c_ctx": nrm(ks[3], (D,), 1.0),
        "ada_w": nrm(ks[4], (DEPTH, D, 6 * D), 0.5 * D ** -0.5),
        "ada_b": nrm(ks[5], (DEPTH, 6 * D), 0.02),
        "norm_mix": 1.0 + nrm(ks[6], (DEPTH, D), 0.02),
        "norm_ffn": 1.0 + nrm(ks[7], (DEPTH, D), 0.02),
        "ffn_w1": nrm(ks[8], (DEPTH, D, D_FF_2), D ** -0.5),
        "ffn_w2": nrm(ks[9], (DEPTH, D_FF_2, D), D_FF_2 ** -0.5),
        "mlstm_w_in": nrm(ks[10], (N_MLSTM, D, A_IN), D ** -0.5),
        "mlstm_gate_b": gate_base + nrm(ks[11], (N_MLSTM, 4, A_HEADS), 0.1),
        "mlstm_head_norm": 1.0 + nrm(ks[12], (N_MLSTM, A_HEADS * A_DV), 0.02),
        "mlstm_w_out": nrm(ks[13], (N_MLSTM, A_HEADS * A_DV, D), (A_HEADS * A_DV) ** -0.5),
        "swa_w_in": nrm(ks[14], (N_SWA, D, SWA_IN), D ** -0.5),
        "swa_sink": nrm(ks[15], (N_SWA, SWA_HEADS), 0.5),
        "swa_w_out": nrm(ks[16], (N_SWA, SWA_HEADS * SWA_DH, D), (SWA_HEADS * SWA_DH) ** -0.5),
        "diff_w_in": nrm(ks[17], (N_DIFF, D, DIFF_IN), D ** -0.5),
        "diff_lambda_q1": nrm(ks[18], (N_DIFF, DIFF_DH), 0.1),
        "diff_lambda_k1": nrm(ks[19], (N_DIFF, DIFF_DH), 0.1),
        "diff_lambda_q2": nrm(ks[20], (N_DIFF, DIFF_DH), 0.1),
        "diff_lambda_k2": nrm(ks[21], (N_DIFF, DIFF_DH), 0.1),
        "diff_head_norm": 1.0 + nrm(ks[22], (N_DIFF, DIFF_HEADS * DIFF_DV), 0.02),
        "diff_w_out": nrm(ks[23], (N_DIFF, DIFF_HEADS * DIFF_DV, D), (DIFF_HEADS * DIFF_DV) ** -0.5),
        "final_norm": 1.0 + nrm(ks[24], (D,), 0.02),
    }

def second_block(x, c, ctx, c_ctx, ada_w, ada_b, norm_mix, norm_ffn, ffn_w1, ffn_w2,
              mlstm_w_in, mlstm_gate_b, mlstm_head_norm, mlstm_w_out,
              swa_w_in, swa_sink, swa_w_out,
              diff_w_in, diff_lambda_q1, diff_lambda_k1, diff_lambda_q2, diff_lambda_k2,
              diff_head_norm, diff_w_out, final_norm):
    n_tok = x.shape[1]
    cos_s, sin_s = _axial_rope_tables(n_tok, SWA_DH)
    cos_d, sin_d = _axial_rope_tables(n_tok, DIFF_DH)
    cond_lat = jax.nn.silu(c)[:, None, :]
    cond_ctx = jax.nn.silu(c_ctx)[None, None, :]
    h, hc = x, ctx
    for i in range(DEPTH):
        kind, slot = i % N_MIXERS, i // N_MIXERS
        need_ctx = i < DEPTH - 1
        mod_l = jnp.split(cond_lat @ ada_w[i] + ada_b[i], 6, axis=-1)
        mod_c = jnp.split(cond_ctx @ ada_w[i] + ada_b[i], 6, axis=-1)
        u = _modulate(_rms_norm(h, norm_mix[i]), mod_l[0], mod_l[1])
        uc = _modulate(_rms_norm(hc, norm_mix[i]), mod_c[0], mod_c[1])
        if kind == 0:
            y, yc = _mlstm_mixer(uc, u, mlstm_w_in[slot], mlstm_gate_b[slot], mlstm_head_norm[slot],
                                 mlstm_w_out[slot], need_ctx)
        elif kind == 1:
            y, yc = _swa_mixer(uc, u, swa_w_in[slot], swa_sink[slot], swa_w_out[slot], cos_s, sin_s, need_ctx)
        else:
            y, yc = _diff_mixer(uc, u, diff_w_in[slot], diff_lambda_q1[slot], diff_lambda_k1[slot],
                                diff_lambda_q2[slot], diff_lambda_k2[slot], diff_head_norm[slot],
                                diff_w_out[slot], cos_d, sin_d, i, need_ctx)
        h = h + mod_l[2] * y
        h = h + mod_l[5] * _sq_relu_mlp(_modulate(_rms_norm(h, norm_ffn[i]), mod_l[3], mod_l[4]),
                                        ffn_w1[i], ffn_w2[i])
        if need_ctx:
            hc = hc + mod_c[2] * yc
            hc = hc + mod_c[5] * _sq_relu_mlp(_modulate(_rms_norm(hc, norm_ffn[i]), mod_c[3], mod_c[4]),
                                              ffn_w1[i], ffn_w2[i])
    return _rms_norm(h, final_norm)


def setup_inputs(seed=0):
    out = dict(first_inputs(seed))
    for name, value in second_inputs(seed + 1).items():
        if name != "x":
            out[name + "_2"] = value
    return out


def reference(
    x, c, ctx, c_ctx, ada_w, ada_b, norm_mix_g, norm_ffn_g, ffn_w1, ffn_w2, dn_w_in, dn_conv_w,
    dn_a_log, dn_dt_bias, dn_norm_g, dn_w_out, gla_w_in, gla_gate_w2, gla_gate_b2, gla_norm_g,
    gla_w_out, attn_w_in, attn_q_norm_g, attn_k_norm_g, attn_w_out, c_2, ctx_2, c_ctx_2,
    ada_w_2, ada_b_2, norm_mix_2, norm_ffn_2, ffn_w1_2, ffn_w2_2, mlstm_w_in_2, mlstm_gate_b_2,
    mlstm_head_norm_2, mlstm_w_out_2, swa_w_in_2, swa_sink_2, swa_w_out_2, diff_w_in_2,
    diff_lambda_q1_2, diff_lambda_k1_2, diff_lambda_q2_2, diff_lambda_k2_2, diff_head_norm_2,
    diff_w_out_2, final_norm_2,
):
    x = first_block(
        x, c, ctx, c_ctx, ada_w, ada_b, norm_mix_g, norm_ffn_g, ffn_w1, ffn_w2, dn_w_in,
        dn_conv_w, dn_a_log, dn_dt_bias, dn_norm_g, dn_w_out, gla_w_in, gla_gate_w2,
        gla_gate_b2, gla_norm_g, gla_w_out, attn_w_in, attn_q_norm_g, attn_k_norm_g, attn_w_out,
    )
    return second_block(
        x, c_2, ctx_2, c_ctx_2, ada_w_2, ada_b_2, norm_mix_2, norm_ffn_2, ffn_w1_2, ffn_w2_2,
        mlstm_w_in_2, mlstm_gate_b_2, mlstm_head_norm_2, mlstm_w_out_2, swa_w_in_2, swa_sink_2,
        swa_w_out_2, diff_w_in_2, diff_lambda_q1_2, diff_lambda_k1_2, diff_lambda_q2_2,
        diff_lambda_k2_2, diff_head_norm_2, diff_w_out_2, final_norm_2,
    )


_drawn_inputs = setup_inputs


def setup_inputs(seed=0):
    import zlib

    import numpy as np

    out = dict(_drawn_inputs(seed))
    spreads = {}
    factors = {'norm_mix_g': 5.443,
     'norm_ffn_g': 4.065,
     'dn_norm_g': 8.0,
     'gla_gate_b2': 6.09,
     'gla_norm_g': 8.0,
     'norm_mix_2': 6.91,
     'norm_ffn_2': 14.699,
     'mlstm_head_norm_2': 149.71,
     'swa_sink_2': 8.0,
     'final_norm_2': 22.319}
    for name, (base, spread) in spreads.items():
        noise = np.random.default_rng([zlib.crc32(name.encode()), seed]).standard_normal(out[name].shape)
        drawn = base * np.exp(spread * noise) if base else spread * noise
        out[name] = jnp.asarray(drawn.astype(out[name].dtype))
    for name, factor in factors.items():
        out[name] = (out[name] * factor).astype(out[name].dtype)
    return out
```

```python
import numpy as np
import concourse.bass as bass
from concourse import mybir
from contextlib import ExitStack

F32 = mybir.dt.float32
ALU = mybir.AluOpType
ACT = mybir.ActivationFunctionType
AXX = mybir.AxisListType.X

P = 128
D = 1024
KT = D // P
NC_ = 256
NX = 512
T = NC_ + NX
NCH = T // P
CCH = NC_ // P
DFF = 4096
EPS = 1e-6
DN_H, DN_G = 16, 4
NG = DN_H // DN_G
LV = 7
NEG = -1.0e30


def build(nc, a, out):
    with ExitStack() as ctx:
        def sb(name, shape, dt=F32):
            return ctx.enter_context(nc.sbuf_tensor(name, shape, dt))

        def sem(name):
            return ctx.enter_context(nc.semaphore(name))

        resid = sb("resid", [P, KT, T])
        h = sb("h", [P, KT, T])
        wring = sb("wring", [P, 2, 4096])
        mods = sb("mods", [P, 4, 48, 2])
        csil = sb("csil", [P, 2, KT, 2])
        adab = sb("adab", [P, 4, 48])
        gains = sb("gains", [P, 9, KT])
        gmod = sb("gmod", [P, KT, 2])
        sqb = sb("sqb", [P, 2, T])
        rnb = sb("rnb", [P, T])
        rstd = rnb
        ident = sb("ident", [P, P])
        ones = sb("ones", [P, P])
        epsc = sb("epsc", [P, 1])
        maskL = sb("maskL", [P, 2, LV, P])
        negm = sb("negm", [P, 2, P])
        tri = sb("tri", [P, 2, P])
        ASZ = 25600
        A_BASE = (nc.sbuf_base + 31) // 32 * 32
        names = []
        A = sb("arena", [P, ASZ])
        ps = ctx.enter_context(nc.psum_tensor("ps", [P, 8, 512], F32))

        arena_base = A_BASE

        def arena(off, *shape):
            n = int(np.prod(shape))
            assert off + n <= ASZ, (off, n)
            names.append(f"phase_buffer{len(names)}")
            t_ = nc.alloc_sbuf_tensor_at(names[-1], [P] + list(shape), F32, offset=A_BASE + 4 * off)
            return t_[tuple(slice(None) for _ in range(len(shape) + 1))]

        const_in = sem("const_in")
        tok_in = sem("tok_in")
        tok2_in = sem("tok2_in")
        landed = [sem("slab0_landed"), sem("slab1_landed")]
        tile_ready = sem("tile_ready")
        pair_free = [sem("pair0_free"), sem("pair1_free")]
        resid_ready = sem("resid_ready")
        h_ready = sem("h_ready")
        out_done = sem("out_done")

        slabs = []
        at = {}
        state = {"tile": 2}

        def phase(name):
            at[name] = (len(slabs), state["tile"])

        def tiles(n):
            state["tile"] += n

        def slab(parts, ntiles):
            assert len(parts) == 2
            state["tile"] += ntiles
            slabs.append((parts, state["tile"] - 1))

        def up(w, c0, n, ntiles, kt=KT):
            v = w.rearrange("(k p) n -> p k n", p=P)
            hk = kt // 2
            slab([(0, hk, n, v[:, 0:hk, c0:c0 + n]), (hk * n, hk, n, v[:, hk:kt, c0:c0 + n])], ntiles)

        def down(w, r0, kt, ntiles):
            v = w[r0:r0 + P * kt, :].rearrange("(k p) n -> p k n", p=P)
            hk = kt // 2
            slab([(0, hk, D, v[:, 0:hk, :]), (hk * D, hk, D, v[:, hk:kt, :])], ntiles)

        MIX = ['dn', 'gla', 'ml', 'swa']
        RESID = {"nm0": 1, "nf0": 2, "nm1": 3, "nf1": 4, "nm2": 6, "nf2": 7, "nm3": 8, "nf3": 9, "nfin": 10}
        NORMS = ["nm0", "nf0", "nm1", "nf1", "nm2", "nf2", "nm3", "nf3", "nfin"]

        def two(w, ca, cb):
            v = w.rearrange("(k p) n -> p k n", p=P)
            slab([(-1, KT, 256, v[:, :, ca:ca + 256]), (-2, KT, 256, v[:, :, cb:cb + 256])], 4)

        def plan_ffn(L, w1, w2):
            phase(f"ffn{L}")
            for n in range(DFF // 512):
                up(w1, 512 * n, 512, 4)
                down(w2, 512 * n, 4, KT)

        def plan_mixer(name, w, wo, groups, c1, c2, c3, c4, vtiles=4):
            phase(name)
            for g in range(groups):
                two(w, c1 + 256 * g, c2 + 256 * g)
                up(w, c3 + 512 * g, 512, vtiles)
                up(w, c4 + 512 * g, 512, 4)
                down(wo, 512 * g, 4, KT)

        if "dn" in MIX:
            plan_mixer("dn", a["dn_w_in"], a["dn_w_out"], NG, 0, 1024, 2048, 4096)
        plan_ffn(0, a["ffn_w1"][0], a["ffn_w2"][0])
        if "gla" in MIX:
            plan_mixer("gla", a["gla_w_in"], a["gla_w_out"], 2, 0, 512, 1024, 2048, NCH)
        plan_ffn(1, a["ffn_w1"][1], a["ffn_w2"][1])
        if "ml" in MIX:
            plan_mixer("ml", a["mlstm_w_in"], a["mlstm_w_out"], 2, 0, 512, 1024, 2048, NCH)
        plan_ffn(2, a["ffn_w1_2"][0], a["ffn_w2_2"][0])
        if "swa" in MIX:
            phase("swa")
            up(a["swa_w_in"], 0, 512, 4)
            up(a["swa_w_in"], 512, 512, 4)
            up(a["swa_k2"], 0, 512, 4)
            up(a["swa_w_in"], 1280, 256, NCH)
            down(a["swa_w_out"], 0, 4, KT)
            down(a["swa_w_out"], 512, 4, KT)
        plan_ffn(3, a["ffn_w1_2"][1], a["ffn_w2_2"][1])

        def lin(i, k, per):
            return k if i is None else i * per + k

        def wslab(s, kt, n):
            return wring[:, s % 2, 0:kt * n].rearrange("p (k n) -> p k n", k=kt)

        def slab_wait(pe, s, i=None, per=0):
            pe.wait_ge(landed[s % 2], lin(i, 32 * (s // 2 + 1), 16 * per))

        def pair_wait(pe, t, i=None, per=0):
            if t >= 2 or i is not None:
                pe.wait_ge(pair_free[t % 2], lin(i, t // 2, per // 2))

        def bank(t, which):
            return ps[:, 2 * (t % 2) + which, :]

        def product_tile(pe, t, kt, lhs, rhs, m=P, i=None, per=0, ctxt=True):
            pair_wait(pe, t, i, per)
            for (b, c0, n) in ([(0, 0, NC_)] if ctxt else []) + [(1, NC_, NX)]:
                for k in range(kt):
                    mm = pe.matmul(bank(t, b)[0:m, 0:n], lhsT=lhs(k), rhs=rhs(k)[:, c0:c0 + n],
                                   start=(k == 0), stop=(k == kt - 1))
            mm.then_inc(tile_ready, 1)

        def up_slab(pe, s, t, src, mt=4, i=None, sper=0, tper=0, ctxt=True):
            slab_wait(pe, s, i, sper)
            w = wslab(s, KT, mt * P)
            for m in range(mt):
                product_tile(pe, t + m, KT, lambda k: w[:, k, m * P:(m + 1) * P],
                             lambda k: src[:, k, :], i=i, per=tper, ctxt=ctxt)

        def down_slab(pe, s, t, src, kt=4, i=None, sper=0, tper=0, ctxt=True):
            slab_wait(pe, s, i, sper)
            w = wslab(s, kt, D)
            for m in range(KT):
                product_tile(pe, t + m, kt, lambda k: w[:, k, m * P:(m + 1) * P],
                             lambda k: src(k), i=i, per=tper, ctxt=ctxt)

        def tile_wait(eng, t, i=None, per=0):
            eng.wait_ge(tile_ready, lin(i, t + 1, per))

        def add_gated(dve, t, L, q, m, i=None, tper=0, ctxt=True):
            tile_wait(dve, t, i, tper)
            if ctxt:
                dve.scalar_tensor_tensor(out=resid[:, m, 0:NC_], in0=bank(t, 0)[:, 0:NC_],
                                         scalar=mods[:, L, 8 * q + m, 1:2], in1=resid[:, m, 0:NC_],
                                         op0=ALU.mult, op1=ALU.add)
            return dve.scalar_tensor_tensor(out=resid[:, m, NC_:T], in0=bank(t, 1)[:, 0:NX],
                                            scalar=mods[:, L, 8 * q + m, 0:1], in1=resid[:, m, NC_:T],
                                            op0=ALU.mult, op1=ALU.add).then_inc(pair_free[t % 2], 1)

        tokbuf = arena(0, NCH, D)
        tr_done = sem("tr_done")
        tr_copied = sem("tr_copied")

        def load_pe(pe, nch, base):
            pe.wait_ge(tok2_in if base else tok_in, 16)
            pe.wait_ge(const_in, CONSTS * 16)
            n = base
            for k in range(KT):
                for g in range((nch + 3) // 4):
                    if n >= 4:
                        pe.wait_ge(tr_copied, n - 3)
                    cs = range(4 * g, min(4 * g + 4, nch))
                    for c in cs:
                        mm = pe.transpose(ps[:, 4 + n % 4, (c % 4) * P:(c % 4 + 1) * P],
                                          tokbuf[:, c, k * P:(k + 1) * P], ident[:, :])
                    mm.then_inc(tr_done, 1)
                    n += 1

        def load_dve(dve, nch, base):
            n = base
            for k in range(KT):
                for g in range((nch + 3) // 4):
                    w = min(4, nch - 4 * g) * P
                    dve.wait_ge(tr_done, n + 1)
                    dve.tensor_copy(resid[:, k, 4 * g * P:4 * g * P + w],
                                    ps[:, 4 + n % 4, 0:w]).then_inc(tr_copied, 1)
                    n += 1

        AW = 384
        adaw = arena(8 * T, 2, KT, AW)
        ada_prod = sem("ada_prod")
        ada_done = sem("ada_done")
        ada_src = [a["ada_w"][0], a["ada_w"][1], a["ada_w_2"][0], a["ada_w_2"][1]]

        ada_landed2 = [sem("ada0_landed"), sem("ada1_landed")]
        adaps = ps[:, 7, 496:502].rearrange("p (m c) -> p m c", c=2)

        def ada_pe(pe, L, i, b):
            pe.wait_ge(ada_landed2[b], lin(i, 16 * (8 * L + 1), 16))
            if L == 0:
                pe.wait_ge(csil_ready, 1)
            pe.wait_ge(ada_done, lin(i, 16 * L + b + 1, 2))
            for m in range(3):
                for k in range(KT):
                    mm = pe.matmul(adaps[:, m, :], lhsT=adaw[:, b, k, m * P:(m + 1) * P],
                                   rhs=csil[:, L // 2, k, :], start=(k == 0), stop=(k == KT - 1))
            mm.then_inc(ada_prod, 1)

        def ada_dve(dve, L, i, b):
            dve.wait_ge(ada_prod, lin(i, 16 * L + b + 1, 2))
            o = mods[:, L, :, :].rearrange("p (s b m) c -> p s b m c", b=2, m=3)
            bb = adab[:, L, :].rearrange("p (s b m) -> p s b m", b=2, m=3)
            dve.tensor_tensor(o[:, bass.ds(i, 1), b, :, :].rearrange("p s m c -> p (s m) c"), adaps,
                              bb[:, bass.ds(i, 1), b, :].rearrange("p s (m c) -> p (s m) c", c=1)
                              .broadcast_to([P, 3, 2]), ALU.add).then_inc(ada_done, 1)

        csil_ready = sem("csil_ready")

        sq_done = sem("sq_done")
        norm_ln = sem("norm_ln")
        norm_mid = sem("norm_mid")
        norm_dve = sem("norm_dve")

        def norm_pe(pe, name, ctxt=True):
            n = NORMS.index(name)
            for k in range(KT):
                pe.wait_ge(sq_done, KT * n + k + 1)
                if ctxt:
                    pe.matmul(ps[:, 4, 0:NC_], lhsT=ones[:, :], rhs=sqb[:, k % 2, 0:NC_],
                              start=(k == 0), stop=(k == KT - 1))
                pe.matmul(ps[:, 5, 0:NX], lhsT=ones[:, :], rhs=sqb[:, k % 2, NC_:T],
                          start=(k == 0), stop=(k == KT - 1)).then_inc(norm_sum, 1)

        norm_sum = sem("norm_sum")

        def norm_act(act, name, ctxt=True):
            n = NORMS.index(name)
            c0 = 0 if ctxt else NC_
            act.preload_act_table_set("natural_log_exp_and_others")
            act.wait_ge(resid_ready, RESID[name])
            for k in range(KT):
                if n or k >= 2:
                    act.wait_ge(norm_sum, KT * n + k - 1)
                act.activation(sqb[:, k % 2, c0:T], resid[:, k, c0:T], ACT.Square).then_inc(sq_done, 1)
            act.wait_ge(norm_sum, KT * (n + 1))
            act.wait_ge(norm_dve, 3 * n)
            if ctxt:
                act.activation(rstd[:, 0:NC_], ps[:, 4, 0:NC_], ACT.Ln, bias=epsc[:, 0:1], scale=1.0 / D)
            act.activation(rstd[:, NC_:T], ps[:, 5, 0:NX], ACT.Ln, bias=epsc[:, 0:1], scale=1.0 / D)\
                .then_inc(norm_ln, 1)
            act.wait_ge(norm_ln, n + 1)
            act.activation(rstd[:, c0:T], rstd[:, c0:T], ACT.Exp, scale=-0.5).then_inc(norm_mid, 1)

        def norm_dve_(dve, name, L, g, q, ctxt=True):
            n = NORMS.index(name)
            c0 = 0 if ctxt else NC_
            dve.wait_ge(norm_dve, 3 * n)
            if L is not None:
                dve.wait_ge(ada_done, 16 * (L + 1) + 1)
                dve.scalar_tensor_tensor(out=gmod[:, :, :], in0=mods[:, L, 8 * (q + 1):8 * (q + 2), :],
                                         scalar=1.0, in1=gains[:, g, :].rearrange("p (k c) -> p k c", c=1)
                                         .broadcast_to([P, KT, 2]), op0=ALU.add, op1=ALU.mult)\
                    .then_inc(norm_dve, 1)
            else:
                dve.tensor_copy(gmod[:, :, :], gains[:, g, :].rearrange("p (k c) -> p k c", c=1)
                                .broadcast_to([P, KT, 2])).then_inc(norm_dve, 1)
            dve.wait_ge(norm_mid, n + 1)
            dve.tensor_tensor(h[:, :, c0:T], resid[:, :, c0:T],
                              rstd[:, c0:T].rearrange("p (k n) -> p k n", k=1)
                              .broadcast_to([P, KT, T - c0]), ALU.mult).then_inc(norm_dve, 1)
            dve.wait_ge(norm_dve, 3 * n + 2)
            for k in range(KT):
                for (cc, lo, hi) in ([(1, 0, NC_)] if ctxt else []) + [(0, NC_, T)]:
                    sh = mods[:, L, 8 * q + k, cc:cc + 1] if L is not None else None
                    last = dve.tensor_scalar(h[:, k, lo:hi], h[:, k, lo:hi], gmod[:, k, cc:cc + 1], sh,
                                             ALU.mult, *([ALU.add] if L is not None else []))
            last.then_inc(norm_dve, 1)

        def h_wait(eng, name):
            eng.wait_ge(norm_dve, 3 * (NORMS.index(name) + 1))

        relu = arena(0, 4, T)
        hid = arena(4 * T, 4, T)
        relu_done = sem("relu_done")
        sqr_done = sem("sqr_done")
        FFN_STEPS = DFF // 512

        def ffn_pe(pe, L, ctxt):
            s, t = at[f"ffn{L}"]
            h_wait(pe, f"nf{L}")
            with pe.Fori(0, FFN_STEPS) as i:
                up_slab(pe, s, t, h, i=i, sper=2, tper=12, ctxt=ctxt)
                if L < 3:
                    ada_pe(pe, L + 1, i, 0)
                    ada_pe(pe, L + 1, i, 1)
                pe.wait_ge(sqr_done, lin(i, 32 * L + 5, 4))
                down_slab(pe, s + 1, t + 4, lambda k: hid[:, k, :], i=i, sper=2, tper=12, ctxt=ctxt)

        def ffn_act(act, L, ctxt):
            t = at[f"ffn{L}"][1]
            with act.Fori(0, FFN_STEPS) as i:
                for m in range(4):
                    tile_wait(act, t + m, i, 12)
                    act.wait_ge(sqr_done, lin(i, 32 * L + 1, 4))
                    if ctxt:
                        act.activation(relu[:, m, 0:NC_], bank(t + m, 0)[:, 0:NC_], ACT.Relu)
                    act.activation(relu[:, m, NC_:T], bank(t + m, 1)[:, 0:NX], ACT.Relu)\
                        .then_inc(pair_free[(t + m) % 2], 1)

        def ffn_pool(pool, L, ctxt):
            t = at[f"ffn{L}"][1]
            c0 = 0 if ctxt else NC_
            with pool.Fori(0, FFN_STEPS) as i:
                pool.wait_ge(tile_ready, lin(i, t, 12))
                for m in range(4):
                    pool.wait_ge(pair_free[(t + m) % 2], lin(i, (t + m) // 2 + 1, 6))
                    pool.tensor_tensor(hid[:, m, c0:T], relu[:, m, c0:T], relu[:, m, c0:T], ALU.mult)\
                        .then_inc(sqr_done, 1)

        def ffn_dve(dve, L, ctxt):
            t = at[f"ffn{L}"][1]
            with dve.Fori(0, FFN_STEPS) as i:
                if L < 3:
                    ada_dve(dve, L + 1, i, 0)
                    ada_dve(dve, L + 1, i, 1)
                for m in range(KT):
                    last = add_gated(dve, t + 4 + m, L, 5, m, i, 12, ctxt)
            t_last = t + 12 * FFN_STEPS - 1
            dve.wait_ge(pair_free[t_last % 2], t_last // 2 + 1)
            dve.wait_ge(pair_free[(t_last - 1) % 2], (t_last - 1) // 2 + 1)
            dve.memset(scr[:, 0:1], 0.0).then_inc(resid_ready, 1)

        scr = sb("scr", [P, 2])
        ostage = arena(0, 4, D)

        class Steps:

            def __init__(self, name, steps):
                self.sem, self.steps, self.n = sem(name), {s: k for k, s in enumerate(steps)}, 0
                assert len(self.steps) == len(steps), name

            def start(self, eng):
                eng.sem_inc(self.sem, 1)

            def done(self, ins, step):
                assert self.steps[step] == self.n % len(self.steps), (step, self.n)
                self.n += 1
                return ins.then_inc(self.sem, 1)

            def wait(self, eng, step, i=None):
                eng.wait_ge(self.sem, lin(i, self.steps[step] + 2, len(self.steps)))

            def passes(self, eng, i):
                eng.wait_ge(self.sem, i * len(self.steps) + 1)

        order = [[0, 1, 2, 3, 4, 5], [1, 0, 5, 4, 3, 2]]
        DK = 6
        dq = arena(0, 4, T)
        dv = arena(4 * T, 4, T)
        do = dv
        dvt = arena(8 * T, NCH, 512)
        dkt = arena(12 * T, NCH, 256)
        off = 14 * T
        pbuf = arena(off, 2, 776)
        wab = arena(off, KT, 64)
        dab = arena(off + 512, NCH, 32)
        dsp = arena(off + 704, NCH, 32)
        nal = arena(off + 896, 32)
        dtb = arena(off + 928, 32)
        cacc = arena(off + 1552, 2, 776)
        off += 3104
        dall = arena(off, DK, 2, NCH, DN_H)
        off += DK * 2 * NCH * DN_H
        dcur = arena(off, DK, 2, NCH, DN_G)
        off += DK * 2 * NCH * DN_G
        ccur = arena(off, 8, 5)
        off += 40
        UB = {}
        for nm in ["eg", "dt", "mt", "at", "x", "xt", "t1", "tmp", "qe", "kt"]:
            UB[nm] = arena(off, 2, 4, P)
            off += 1024
        UB["ns"] = UB["dt"]
        US = UB["s"] = sb("state", [P, 2, 4, P])
        convw = sb("convw", [P, 32, 5])
        zbuf = cacc

        def dsteps():
            pe, act, dve, pool = [], [], [], []
            dve.append("cur")
            for n in range(8):
                act.append(("silu", n))
                dve += [("conv", n, k) for k in range(5)]
            for n in range(4):
                act += [("sq", n), ("ln", n), ("rn", n)]
                pe.append(("ss", n))
                dve.append(("qkn", n))
            for n in range(NCH + 3):
                pe.append(("tr", n))
                act.append(("trc", n))
            dve.append("s0")
            for u in range(NCH):
                for st in ["G", "K"]:
                    pe += [(st, u, d) for d in range(2)]
                act += [("eg", u, d) for d in range(2)]
                for d in range(2):
                    dve += [("gd", u, d), ("gm", u, d)]
                act += [("dt", u, d) for d in range(2)]
                for d in range(2):
                    dve += [("qe", u, d), ("kd", u, d), ("mt", u, d), ("at", u, d)]
                pool += [("kt", u, d) for d in range(2)]
                for l in range(LV):
                    pool += [("ns", u, d, l) for d in range(2)]
                    pe += [("T1", u, d, l) for d in range(2)]
                    if l:
                        act += [("t1", u, d, l) for d in range(2)]
                        for d in range(2):
                            pe += ([("T2", u, d, l)] if l < LV - 1 else []) + [("T3", u, d, l)]
                    for d in range(2):
                        dve += ([("x", u, d, l)] if l < LV - 1 else []) + [("xt", u, d, l)]
                pe += [("KS", u, d) for d in range(2)]
                for d in range(2):
                    dve += [("r1", u, d), ("r2", u, d)]
                pe += [("XR", u, d) for d in range(2)]
                dve += [("vn", u, d) for d in range(2)]
                for d in range(2):
                    pe += [("O", u, d), ("DS", u, d)]
                for d in range(2):
                    dve += [("o", u, d), ("s1", u, d), ("s2", u, d)]
            for n in range(4):
                act += [("osq", n), ("oln", n), ("orn", n)]
                pe.append(("oss", n))
                dve.append(("on", n))
            dve += [("oz", n) for n in range(4)]
            dve.append("end")
            return pe, act, dve, pool

        dS = dict(zip(["pe", "act", "dve", "pool"], [Steps("delta_" + n, s) for n, s in
                                                      zip(["pe", "act", "dve", "pool"], dsteps())]))
        dprep = sem("delta_prep_pe")
        dprep_v = sem("delta_prep_dve")
        dprep_a = sem("delta_prep_act")
        dprep_in = sem("delta_weights_in")

        def four(ap2, u=None):
            return ap2.rearrange("p (h n) -> p h n", n=1).broadcast_to([P, 4, P])

        def spread(m):
            return m.rearrange("p (h n) -> p h n", h=1).broadcast_to([P, 4, P])

        def pairs(x):
            return x.rearrange("p h (g n) -> p h g n", g=1).broadcast_to([P, 2, 2, P])

        def as22(x):
            return x.rearrange("p (h g) n -> p h g n", g=2)

        def bk(b):
            return ps[:, b, :].rearrange("p (h n) -> p h n", h=4)

        def cs(c):
            return slice(c * P, (c + 1) * P)

        def others(eng, S, me, i):
            for n in S:
                if n != me:
                    S[n].passes(eng, i)

        def delta_pe(pe):
            s, t = at["dn"]
            h_wait(pe, "nm0")
            pe.wait_ge(dprep_in, 48)
            for c in range(NCH):
                for k in range(KT):
                    mm = pe.matmul(ps[:, 4, c * 64:(c + 1) * 64], lhsT=h[:, k, cs(c)], rhs=wab[:, k, :],
                                   start=(k == 0), stop=(k == KT - 1))
            mm.then_inc(dprep, 1)
            pe.wait_ge(dprep_v, 4)
            for d in range(2):
                g = dall[:, 0, d, :, :]
                pe.matmul(ps[:, 5, 96 * d:96 * d + 96], lhsT=tri[:, d, :], rhs=g, start=True, stop=True)
                mm = pe.matmul(ps[:, 5, 192 + 96 * d:288 + 96 * d], lhsT=ones[:, :], rhs=g, start=True, stop=True)
            mm.then_inc(dprep, 1)
            S = dS
            me = S["pe"]
            me.start(pe)
            with pe.Fori(0, NG) as i:
                others(pe, S, "pe", i)
                up_slab(pe, s, t, h, i=i, sper=4, tper=20)
                up_slab(pe, s + 1, t + 4, h, i=i, sper=4, tper=20)
                for n in range(4):
                    S["act"].wait(pe, ("sq", n), i)
                    b = 4 + 2 * (n % 2)
                    if n >= 2:
                        S["act"].wait(pe, ("ln", n - 2), i)
                    pe.matmul(ps[:, b, 0:NC_], lhsT=ones[:, :], rhs=sqb[:, n % 2, 0:NC_], start=True, stop=True)
                    me.done(pe.matmul(ps[:, b + 1, 0:NX], lhsT=ones[:, :], rhs=sqb[:, n % 2, NC_:T],
                                      start=True, stop=True), ("ss", n))
                S["act"].wait(pe, ("ln", 3), i)
                S["act"].wait(pe, ("silu", 7), i)
                for n in range(NCH + 3):
                    b = 4 + n % 4
                    if n >= 4:
                        S["act"].wait(pe, ("trc", n - 4), i)
                    if n == NCH:
                        S["dve"].wait(pe, ("qkn", 3), i)
                    for m in range(4):
                        if n < NCH:
                            src = dv[:, m, cs(n)]
                        else:
                            src = dq[:, 2 + m % 2, cs(2 * (n - NCH) + m // 2)]
                        mm = pe.transpose(ps[:, b, cs(m)], src, ident[:, :])
                    me.done(mm, ("tr", n))
                S["act"].wait(pe, ("trc", NCH + 2), i)
                for u in range(NCH):
                    for d in range(2):
                        c = order[d][u]
                        if u:
                            S["dve"].wait(pe, ("s2", u - 1, d), i)
                        for hh in range(4):
                            mm = pe.matmul(ps[:, 4 + 2 * d, cs(hh)],
                                           lhsT=dcur[:, 0, d, c, hh:hh + 1].broadcast_to([P, P]),
                                           rhs=tri[:, d, :], start=True, stop=True)
                        me.done(mm, ("G", u, d))
                    for d in range(2):
                        c = order[d][u]
                        for kh in range(2):
                            for w in range(2):
                                mm = pe.matmul(ps[:, 5 + 2 * d, cs(2 * w + kh)], lhsT=dq[:, 2 + kh, cs(c)],
                                               rhs=dq[:, (2 if w == 0 else 0) + kh, cs(c)], start=True, stop=True)
                        me.done(mm, ("K", u, d))
                    for l in range(LV):
                        for d in range(2):
                            S["pool"].wait(pe, ("ns", u, d, l), i)
                            if l == 0:
                                S["act"].wait(pe, ("eg", u, d), i)
                                S["dve"].wait(pe, ("gd", u, d), i)
                            else:
                                S["dve"].wait(pe, ("xt", u, d, l - 1), i)
                            for hh in range(4):
                                o = ps[:, 4 + 2 * d, cs(hh)]
                                if l == 0:
                                    mm = pe.transpose(o, UB["ns"][:, d, hh, :], ident[:, :])
                                else:
                                    mm = pe.matmul(o, lhsT=UB["ns"][:, d, hh, :], rhs=UB["x"][:, d, hh, :],
                                                   start=True, stop=True)
                            me.done(mm, ("T1", u, d, l))
                        if not l:
                            continue
                        for d in range(2):
                            S["act"].wait(pe, ("t1", u, d, l), i)
                            if l == 1:
                                S["dve"].wait(pe, ("at", u, d), i)
                            if l < LV - 1:
                                for hh in range(4):
                                    mm = pe.matmul(ps[:, 5 + 2 * d, cs(hh)], lhsT=UB["xt"][:, d, hh, :],
                                                   rhs=UB["t1"][:, d, hh, :], start=True, stop=True)
                                me.done(mm, ("T2", u, d, l))
                            for hh in range(4):
                                mm = pe.matmul(ps[:, 4 + 2 * d, cs(hh)], lhsT=UB["t1"][:, d, hh, :],
                                               rhs=UB["xt"][:, d, hh, :], start=True, stop=True)
                            me.done(mm, ("T3", u, d, l))
                    for d in range(2):
                        c = order[d][u]
                        if u == 0:
                            S["dve"].wait(pe, "s0", i)
                        for hh in range(4):
                            mm = pe.matmul(ps[:, 5 + 2 * d, cs(hh)], lhsT=dq[:, 2 + hh // 2, cs(c)],
                                           rhs=US[:, d, hh, :], start=True, stop=True)
                        me.done(mm, ("KS", u, d))
                    for d in range(2):
                        S["dve"].wait(pe, ("r2", u, d), i)
                        for hh in range(4):
                            mm = pe.matmul(ps[:, 4 + 2 * d, cs(hh)], lhsT=UB["xt"][:, d, hh, :],
                                           rhs=UB["tmp"][:, d, hh, :], start=True, stop=True)
                        me.done(mm, ("XR", u, d))
                    for d in range(2):
                        S["dve"].wait(pe, ("vn", u, d), i)
                        S["pool"].wait(pe, ("kt", u, d), i)
                        for hh in range(4):
                            pe.matmul(ps[:, 5 + 2 * d, cs(hh)], lhsT=US[:, d, hh, :],
                                      rhs=UB["qe"][:, d, hh, :], start=True, stop=False)
                            mm = pe.matmul(ps[:, 5 + 2 * d, cs(hh)], lhsT=UB["t1"][:, d, hh, :],
                                           rhs=UB["at"][:, d, hh, :], start=False, stop=True)
                        me.done(mm, ("O", u, d))
                        for hh in range(4):
                            mm = pe.matmul(ps[:, 4 + 2 * d, cs(hh)], lhsT=UB["kt"][:, d, hh, :],
                                           rhs=UB["t1"][:, d, hh, :], start=True, stop=True)
                        me.done(mm, ("DS", u, d))
                for n in range(4):
                    S["act"].wait(pe, ("osq", n), i)
                    b = 4 + 2 * (n % 2)
                    if n == 0:
                        for d in range(2):
                            S["dve"].wait(pe, ("s2", NCH - 1, d), i)
                    if n >= 2:
                        S["act"].wait(pe, ("oln", n - 2), i)
                    pe.matmul(ps[:, b, 0:NC_], lhsT=ones[:, :], rhs=sqb[:, n % 2, 0:NC_], start=True, stop=True)
                    me.done(pe.matmul(ps[:, b + 1, 0:NX], lhsT=ones[:, :], rhs=sqb[:, n % 2, NC_:T],
                                      start=True, stop=True), ("oss", n))
                up_slab(pe, s + 2, t + 8, h, i=i, sper=4, tper=20)
                S["dve"].wait(pe, ("oz", 3), i)
                down_slab(pe, s + 3, t + 12, lambda k: do[:, k, :], i=i, sper=4, tper=20)

        def delta_act(act):
            t = at["dn"][1]
            act.wait_ge(dprep_in, 48)
            act.activation(nal, nal, ACT.Exp).then_inc(dprep_a, 1)
            act.wait_ge(dprep_v, 1)
            act.activation(dall[:, 5, :, :, :].rearrange("p d c h -> p c d h"),
                           ps[:, 4, 0:384].rearrange("p (c k) -> p c k", c=NCH)[:, :, 32:64]
                           .rearrange("p c (d h) -> p c d h", d=2), ACT.Sigmoid).then_inc(dprep_a, 1)
            act.wait_ge(dprep_v, 2)
            act.activation(dsp, dsp, ACT.Exp).then_inc(dprep_a, 1)
            act.wait_ge(dprep_a, 3)
            act.activation(dsp, dsp, ACT.Ln, bias=1.0).then_inc(dprep_a, 1)
            act.wait_ge(dprep, 2)
            act.activation(dall[:, 1, :, :, :].rearrange("p d c h -> p (d c h)"), ps[:, 5, 0:192],
                           ACT.Copy).then_inc(dprep_a, 1)
            act.activation(dall[:, 2, :, :, :].rearrange("p d c h -> p (d c h)"), ps[:, 5, 0:192],
                           ACT.Exp).then_inc(dprep_a, 1)
            act.activation(dall[:, 3, :, :, :].rearrange("p d c h -> p (d c h)"), ps[:, 5, 192:384],
                           ACT.Exp).then_inc(dprep_a, 1)
            act.wait_ge(dprep_v, 5)
            act.activation(dall[:, 4, :, :, :].rearrange("p d c h -> p (d c h)"),
                           dall[:, 4, :, :, :].rearrange("p d c h -> p (d c h)"), ACT.Exp).then_inc(dprep_a, 1)
            act.wait_ge(dprep_v, 6)
            S = dS
            me = S["act"]
            me.start(act)
            with act.Fori(0, NG) as i:
                others(act, S, "act", i)
                for n in range(9):
                    if n < 8:
                        tile_wait(act, t + n, i, 20)
                        if n >= 2:
                            S["dve"].wait(act, ("conv", n - 2, 4), i)
                        act.activation(pbuf[:, n % 2, 2:2 + NC_], bank(t + n, 0)[:, 0:NC_], ACT.Copy)
                        act.activation(pbuf[:, n % 2, 262:262 + NX], bank(t + n, 1)[:, 0:NX], ACT.Copy)\
                            .then_inc(pair_free[(t + n) % 2], 1)
                    if n:
                        m = n - 1
                        S["dve"].wait(act, ("conv", m, 4), i)
                        dst = dq[:, m, :] if m < 4 else dv[:, m - 4, :]
                        act.activation(dst[:, 0:NC_], cacc[:, m % 2, 0:NC_], ACT.Silu)
                        me.done(act.activation(dst[:, NC_:T], cacc[:, m % 2, 260:260 + NX], ACT.Silu), ("silu", m))
                act.preload_act_table_set("natural_log_exp_and_others")
                for n in range(4):
                    me_norm(act, S, i, n, dq[:, n, :], ("sq", n), ("ss", n), ("ln", n), ("rn", n), 1.0,
                            [("silu", 3)], ("qkn", n - 1) if n else None)
                for n in range(NCH + 3):
                    S["pe"].wait(act, ("tr", n), i)
                    if n < NCH:
                        o = dvt[:, n, :]
                    else:
                        o = dkt[:, 2 * (n - NCH):2 * (n - NCH) + 2, :].rearrange("p c n -> p (c n)")
                    me.done(act.activation(o, ps[:, 4 + n % 4, :], ACT.Copy), ("trc", n))
                for u in range(NCH):
                    for d in range(2):
                        S["dve"].wait(act, ("gd", u, d), i)
                        me.done(act.activation(UB["eg"][:, d, :, :], bk(4 + 2 * d), ACT.Exp), ("eg", u, d))
                    for d in range(2):
                        S["dve"].wait(act, ("gm", u, d), i)
                        me.done(act.activation(UB["dt"][:, d, :, :], UB["tmp"][:, d, :, :], ACT.Exp), ("dt", u, d))
                    for l in range(1, LV):
                        for d in range(2):
                            S["pe"].wait(act, ("T1", u, d, l), i)
                            me.done(act.activation(UB["t1"][:, d, :, :], bk(4 + 2 * d), ACT.Copy), ("t1", u, d, l))
                for n in range(4):
                    me_norm(act, S, i, n, do[:, n, :], ("osq", n), ("oss", n), ("oln", n), ("orn", n), 1.0 / P,
                            [], ("on", n - 1) if n else None,
                            [("o", NCH - 1, d) for d in range(2)])
                for n in range(4):
                    tile_wait(act, t + 8 + n, i, 20)
                    if n >= 2:
                        S["dve"].wait(act, ("oz", n - 2), i)
                    act.activation(zbuf[:, n % 2, 0:NC_], bank(t + 8 + n, 0)[:, 0:NC_], ACT.Silu)
                    act.activation(zbuf[:, n % 2, NC_:T], bank(t + 8 + n, 1)[:, 0:NX], ACT.Silu)\
                        .then_inc(pair_free[(t + n) % 2], 1)


        def me_norm(act, S, i, n, src, sq, ss, ln, rn, scale, mine, used, dwaits=()):
            for w in mine:
                S["act"].wait(act, w, i)
            for w in dwaits:
                S["dve"].wait(act, w, i)
            if n >= 2:
                S["pe"].wait(act, (ss[0], n - 2), i)
            S["act"].done(act.activation(sqb[:, n % 2, :], src, ACT.Square), sq)
            S["pe"].wait(act, ss, i)
            if used:
                S["dve"].wait(act, used, i)
            b = 4 + 2 * (n % 2)
            act.activation(rnb[:, 0:NC_], ps[:, b, 0:NC_], ACT.Ln, bias=epsc[:, 0:1], scale=scale)
            S["act"].done(act.activation(rnb[:, NC_:T], ps[:, b + 1, 0:NX], ACT.Ln, bias=epsc[:, 0:1],
                                         scale=scale), ln)
            S["act"].wait(act, ln, i)
            S["act"].done(act.activation(rnb[:, :], rnb[:, :], ACT.Exp, scale=-0.5), rn)

        def delta_dve(dve):
            t = at["dn"][1]
            dve.wait_ge(dprep_in, 48)
            dve.wait_ge(dprep, 1)
            v = dve
            x = ps[:, 4, 0:384].rearrange("p (c k) -> p c k", c=NCH)[:, :, 0:32]
            v.tensor_tensor(dab[:, :, 0:32], x, dtb.rearrange("p (c k) -> p c k", c=1)
                            .broadcast_to([P, NCH, 32]), ALU.add).then_inc(dprep_v, 1)
            v.wait_ge(dprep_v, 1)
            v.scalar_tensor_tensor(out=dsp, in0=dab[:, :, 0:32], scalar=-1.0, in1=dab[:, :, 0:32],
                                   op0=ALU.mult, op1=ALU.min).then_inc(dprep_v, 1)
            v.wait_ge(dprep_a, 4)
            v.scalar_tensor_tensor(out=dsp, in0=dab[:, :, 0:32], scalar=0.0, in1=dsp,
                                   op0=ALU.max, op1=ALU.add).then_inc(dprep_v, 1)
            v.wait_ge(dprep_v, 3)
            for d in range(2):
                ins = v.scalar_tensor_tensor(out=dall[:, 0, d, :, :], in0=dsp[:, :, 16 * d:16 * d + 16],
                                             scalar=-1.0,
                                             in1=nal[:, 16 * d:16 * d + 16].rearrange("p (c h) -> p c h", c=1)
                                             .broadcast_to([P, NCH, DN_H]), op0=ALU.mult, op1=ALU.mult)
            ins.then_inc(dprep_v, 1)
            v.wait_ge(dprep_a, 7)
            v.tensor_tensor(dall[:, 4, :, :, :].rearrange("p d c h -> p (d c h)"), ps[:, 5, 192:384],
                            dall[:, 1, :, :, :].rearrange("p d c h -> p (d c h)"), ALU.subtract)\
                .then_inc(dprep_v, 1)
            v.wait_ge(dprep_v, 5)
            v.memset(pbuf, 0.0).then_inc(dprep_v, 1)
            v.wait_ge(dprep_a, 8)
            v.wait_ge(dprep_v, 6)
            S = dS
            me = S["dve"]
            me.start(v)
            with dve.Fori(0, NG) as i:
                others(v, S, "dve", i)
                v.wait_ge(dprep_v, 6)
                v.tensor_copy(dcur.rearrange("p k d c h -> p (k d c) h"),
                              dall.rearrange("p k d c h -> p (k d c) h")[:, :, bass.ds(i * 4, 4)])
                v.tensor_copy(ccur[:, 0:2, :], convw[:, bass.ds(i * 2, 2), :])
                v.tensor_copy(ccur[:, 2:4, :], convw[:, bass.ds(i * 2 + 8, 2), :])
                me.done(v.tensor_copy(ccur[:, 4:8, :], convw[:, bass.ds(i * 4 + 16, 4), :]), "cur")
                me.wait(v, "cur", i)
                W = 772
                for n in range(8):
                    v.wait_ge(pair_free[(t + n) % 2], lin(i, (t + n) // 2 + 1, 10))
                    if n >= 2:
                        S["act"].wait(v, ("silu", n - 2), i)
                    for k in range(5):
                        o, p_ = cacc[:, n % 2, 0:W], pbuf[:, n % 2, k:k + W]
                        if k == 0:
                            ins = v.tensor_scalar(o, p_, ccur[:, n, 0:1], None, ALU.mult)
                        else:
                            me.wait(v, ("conv", n, k - 1), i)
                            ins = v.scalar_tensor_tensor(out=o, in0=p_, scalar=ccur[:, n, k:k + 1], in1=o,
                                                         op0=ALU.mult, op1=ALU.add)
                        me.done(ins, ("conv", n, k))
                for n in range(4):
                    S["act"].wait(v, ("rn", n), i)
                    me.done(v.scalar_tensor_tensor(out=dq[:, n, :], in0=dq[:, n, :],
                                                   scalar=float(P) ** -0.5 if n < 2 else 1.0, in1=rnb[:, :],
                                                   op0=ALU.mult, op1=ALU.mult), ("qkn", n))
                S["pe"].wait(v, ("tr", NCH - 1), i)
                v.memset(do, 0.0)
                me.done(v.memset(US[:, :, :, :], 0.0), "s0")
                me.wait(v, "s0", i)
                S["act"].wait(v, ("trc", NCH + 2), i)
                for u in range(NCH):
                    for d in range(2):
                        c = order[d][u]
                        S["pe"].wait(v, ("G", u, d), i)
                        me.done(v.tensor_tensor(UB["tmp"][:, d, :, :], bk(4 + 2 * d), four(dcur[:, 1, d, c, :]),
                                                ALU.subtract), ("gd", u, d))
                        me.wait(v, ("gd", u, d), i)
                        me.done(v.tensor_tensor(UB["tmp"][:, d, :, :], UB["tmp"][:, d, :, :],
                                                spread(negm[:, d, :]), ALU.add), ("gm", u, d))
                    for d in range(2):
                        c = order[d][u]
                        S["act"].wait(v, ("eg", u, d), i)
                        me.done(v.tensor_tensor(as22(UB["qe"][:, d, :, :]), pairs(dq[:, 0:2, cs(c)]),
                                                as22(UB["eg"][:, d, :, :]), ALU.mult), ("qe", u, d))
                        S["act"].wait(v, ("dt", u, d), i)
                        S["pe"].wait(v, ("K", u, d), i)
                        kb = bk(5 + 2 * d)
                        me.done(v.tensor_tensor(as22(UB["mt"][:, d, :, :]), pairs(kb[:, 0:2, :]),
                                                as22(UB["dt"][:, d, :, :]), ALU.mult), ("kd", u, d))
                        me.wait(v, ("kd", u, d), i)
                        me.done(v.tensor_tensor(UB["mt"][:, d, :, :], UB["mt"][:, d, :, :],
                                                four(dcur[:, 5, d, c, :]), ALU.mult), ("mt", u, d))
                        me.done(v.tensor_tensor(as22(UB["at"][:, d, :, :]), pairs(kb[:, 2:4, :]),
                                                as22(UB["dt"][:, d, :, :]), ALU.mult), ("at", u, d))
                    for l in range(LV):
                        for d in range(2):
                            if l == 0:
                                S["pe"].wait(v, ("T1", u, d, 0), i)
                                me.done(v.tensor_tensor(UB["x"][:, d, :, :], spread(ident[:, :]), bk(4 + 2 * d),
                                                        ALU.subtract), ("x", u, d, 0))
                                me.done(v.tensor_tensor(UB["xt"][:, d, :, :], spread(ident[:, :]),
                                                        UB["ns"][:, d, :, :], ALU.subtract), ("xt", u, d, 0))
                                continue
                            me.wait(v, ("xt", u, d, l - 1), i)
                            if l < LV - 1:
                                S["pe"].wait(v, ("T2", u, d, l), i)
                                me.done(v.tensor_tensor(UB["x"][:, d, :, :], UB["x"][:, d, :, :], bk(5 + 2 * d),
                                                        ALU.subtract), ("x", u, d, l))
                            S["pe"].wait(v, ("T3", u, d, l), i)
                            me.done(v.tensor_tensor(UB["xt"][:, d, :, :], UB["xt"][:, d, :, :], bk(4 + 2 * d),
                                                    ALU.subtract), ("xt", u, d, l))
                    for d in range(2):
                        c = order[d][u]
                        S["pe"].wait(v, ("KS", u, d), i)
                        S["act"].wait(v, ("dt", u, d), i)
                        me.done(v.tensor_tensor(UB["tmp"][:, d, :, :], bk(5 + 2 * d), four(dcur[:, 2, d, c, :]),
                                                ALU.mult), ("r1", u, d))
                        me.wait(v, ("r1", u, d), i)
                        me.done(v.tensor_tensor(UB["tmp"][:, d, :, :], UB["tmp"][:, d, :, :],
                                                dvt[:, c, :].rearrange("p (h n) -> p h n", h=4),
                                                ALU.subtract), ("r2", u, d))
                    for d in range(2):
                        c = order[d][u]
                        S["pe"].wait(v, ("XR", u, d), i)
                        me.done(v.scalar_tensor_tensor(out=UB["t1"][:, d, :, :], in0=bk(4 + 2 * d), scalar=-1.0,
                                                       in1=four(dcur[:, 5, d, c, :]), op0=ALU.mult,
                                                       op1=ALU.mult), ("vn", u, d))
                    for d in range(2):
                        c = order[d][u]
                        S["pe"].wait(v, ("O", u, d), i)
                        if d:
                            me.wait(v, ("o", u, 0), i)
                        if u:
                            me.wait(v, ("o", u - 1, 1), i)
                        me.done(v.tensor_tensor(do[:, :, cs(c)], do[:, :, cs(c)], bk(5 + 2 * d), ALU.add),
                                ("o", u, d))
                        S["pe"].wait(v, ("DS", u, d), i)
                        me.done(v.tensor_tensor(US[:, d, :, :], US[:, d, :, :], four(dcur[:, 3, d, c, :]),
                                                ALU.mult), ("s1", u, d))
                        me.wait(v, ("s1", u, d), i)
                        me.done(v.tensor_tensor(US[:, d, :, :], US[:, d, :, :], bk(4 + 2 * d), ALU.add),
                                ("s2", u, d))
                for n in range(4):
                    S["act"].wait(v, ("orn", n), i)
                    me.wait(v, ("s2", NCH - 1, 1), i)
                    me.done(v.scalar_tensor_tensor(out=do[:, n, :], in0=do[:, n, :], scalar=dng[:, 0:1],
                                                   in1=rnb[:, :], op0=ALU.mult, op1=ALU.mult), ("on", n))
                for n in range(4):
                    me.wait(v, ("on", n), i)
                    v.wait_ge(pair_free[(t + n) % 2], lin(i, (t + 8 + n) // 2 + 1, 10))
                    me.done(v.tensor_tensor(do[:, n, :], do[:, n, :], zbuf[:, n % 2, 0:T], ALU.mult), ("oz", n))
                for m in range(KT):
                    add_gated(v, t + 12 + m, 0, 2, m, i, 20)
                end_of_updates(v, t + 19, i, 10)
                me.done(v.memset(scr[:, 0:1], 0.0), "end")
            me.passes(v, NG)
            v.memset(scr[:, 1:2], 0.0).then_inc(resid_ready, 1)

        dng = sb("dng", [P, 1])

        def end_of_updates(dve, t, i=None, per=0):
            for q in (t, t - 1):
                dve.wait_ge(pair_free[q % 2], lin(i, q // 2 + 1, per))

        def delta_pool(pool):
            h_wait(pool, "nm0")
            for dst, src in ((wab, a["dn_w_in"][:, 6144:6208].rearrange("(k p) n -> p k n", p=P)),
                             (nal, a["dal"].partition_broadcast(P)), (dtb, a["ddt"].partition_broadcast(P))):
                pool.dma_start(dst, src).then_inc(dprep_in, 16)
            S = dS
            me = S["pool"]
            me.start(pool)
            with pool.Fori(0, NG) as i:
                others(pool, S, "pool", i)
                S["dve"].wait(pool, "cur", i)
                S["act"].wait(pool, ("trc", NCH + 2), i)
                for u in range(NCH):
                    for d in range(2):
                        c = order[d][u]
                        if u:
                            S["pe"].wait(pool, ("DS", u - 1, d), i)
                        me.done(pool.tensor_tensor(as22(UB["kt"][:, d, :, :]),
                                                   pairs(dkt[:, c, :].rearrange("p (h n) -> p h n", h=2)),
                                                   as22(four(dcur[:, 4, d, c, :])), ALU.mult), ("kt", u, d))
                    for l in range(LV):
                        for d in range(2):
                            if l == 0:
                                S["dve"].wait(pool, ("at", u, d), i)
                            else:
                                S["pe"].wait(pool, ("T1", u, d, l - 1), i)
                            if l == 1:
                                S["dve"].wait(pool, ("xt", u, d, 0), i)
                            me.done(pool.tensor_tensor(UB["ns"][:, d, :, :], UB["mt"][:, d, :, :],
                                                       spread(maskL[:, d, l, :]), ALU.mult), ("ns", u, d, l))

        gq = arena(0, 2, T)
        gk = arena(2 * T, 2, T)
        gv = arena(4 * T, NCH, 512)
        gB = arena(8 * T, 4, T)
        go = arena(12 * T, 4, T)
        off = 16 * T
        gx = arena(off, 2, T)
        glow = arena(off + 2 * T, 2, T)
        gzb = arena(off + 4 * T, 2, T)
        off += 6 * T
        gw2 = arena(off, 2, 512)
        gw2c = arena(off + 1024, 2, 256)
        gwl = arena(off + 1536, KT, 32)
        off += 1792
        gS = arena(off, 2, 2, 256)
        GU = {}
        off += 1024
        for nm in ["e", "kt", "ktm", "eb", "qe", "df", "ql", "kl", "at", "pm"]:
            GU[nm] = arena(off, 2, 2, P)
            off += 512
        gb2 = sb("gb2", [P, 2, 4])
        gb2c = sb("gb2c", [P, 2, 2])
        gng = sb("gng", [P, 2])
        rst = arena(off, T)
        gin = sem("gla_weights_in")
        gp = sem("gla_low_done")
        gpa = sem("gla_low_copied")

        def gsteps():
            pe, act, dve = [], [], ["cur"]
            for n in range(4):
                pe.append(("lg", n))
                dve += [("x", n), ("na", n), ("t", n), ("sc", n)]
                act += [("e1", n), ("l1", n)]
            dve.append("s0")
            for u in range(NCH):
                dve += [("tl", u, d) for d in range(2)]
                for d in range(2):
                    act += [("te", u, d), ("eb", u, d)]
                    dve.append(("kt", u, d))
                    pe.append(("TK", u, d))
                    act.append(("tkc", u, d))
                if u >= CCH:
                    dve += [("qe", u, d) for d in range(2)]
                    for l in range(LV + 1):
                        for d in range(2):
                            if l < LV:
                                dve += [("df", u, l, d), ("ab", u, l, d)]
                                act.append(("ex", u, l, d))
                        for d in range(2):
                            if l < LV:
                                dve += [("ql", u, l, d), ("kl", u, l, d)]
                            pe.append(("P", u, l, d))
                        for d in range(2):
                            dve += [("pm", u, l, d), ("ac", u, l, d)]
                    pe += [("O", u, d) for d in range(2)]
                    dve += [("o", u, d) for d in range(2)]
                pe += [("DS", u, d) for d in range(2)]
                dve += [("s", u, d) for d in range(2)]
            for n in range(2):
                act += [("sq", 2 * n), ("sq", 2 * n + 1), ("ln", n), ("rn", n)]
                pe += [("ss", n)]
                dve += [("on", 2 * n), ("on", 2 * n + 1)]
            dve += [("oz", n) for n in range(4)] + ["end"]
            return pe, act, dve

        gSt = dict(zip(["pe", "act", "dve"], [Steps("gla_" + n, s) for n, s in zip(["pe", "act", "dve"], gsteps())]))

        def mine(S, me, eng, i):
            s_ = S[me]
            eng.wait_ge(s_.sem, lin(i, s_.n % len(s_.steps) + 1, len(s_.steps)))

        def v_tiles(pe, s, t, i, sper, tper):
            slab_wait(pe, s, i, sper)
            w = wslab(s, KT, 512)
            for c in range(NCH):
                pair_wait(pe, t + c, i, tper)
                for k in range(KT):
                    mm = pe.matmul(bank(t + c, 1), lhsT=h[:, k, cs(c)], rhs=w[:, k, :],
                                   start=(k == 0), stop=(k == KT - 1))
                mm.then_inc(tile_ready, 1)

        def gla_pe(pe):
            s, t = at["gla"]
            h_wait(pe, "nm1")
            pe.wait_ge(gin, 48)
            for d in range(2):
                for (b, c0, n) in ((4, 0, NC_), (5, NC_, NX)):
                    for k in range(KT):
                        mm = pe.matmul(ps[0:16, b + 2 * d, 0:n], lhsT=gwl[:, k, 16 * d:16 * d + 16],
                                       rhs=h[:, k, c0:c0 + n], start=(k == 0), stop=(k == KT - 1))
            mm.then_inc(gp, 1)
            S = gSt
            me = S["pe"]
            me.start(pe)
            with pe.Fori(0, 2) as i:
                others(pe, S, "pe", i)
                up_slab(pe, s, t, h, i=i, sper=4, tper=22)
                v_tiles(pe, s + 1, t + 4, i, 4, 22)
                pe.wait_ge(gpa, 1)
                S["dve"].wait(pe, "cur", i)
                for n in range(4):
                    d, hh, b = n // 2, n % 2, 4 + 2 * (n % 2)
                    if n >= 2:
                        S["dve"].wait(pe, ("x", n - 2), i)
                    for (bb, c0, w) in ((b, 0, NC_), (b + 1, NC_, NX)):
                        mm = pe.matmul(ps[:, bb, 0:w], lhsT=gw2c[0:16, d, hh * P:(hh + 1) * P],
                                       rhs=glow[0:16, d, c0:c0 + w], start=True, stop=True)
                    me.done(mm, ("lg", n))
                S["dve"].wait(pe, "s0", i)
                for n in range(2):
                    pe.wait_ge(pair_free[(t + n) % 2], lin(i, (t + 8 + n) // 2 + 1, 11))
                for u in range(NCH):
                    for d in range(2):
                        S["dve"].wait(pe, ("kt", u, d), i)
                        if u:
                            S["dve"].wait(pe, ("s", u - 1, d), i)
                        for hh in range(2):
                            mm = pe.transpose(ps[:, 4 + 2 * d, cs(hh)], GU["kt"][:, d, hh, :], ident[:, :])
                        me.done(mm, ("TK", u, d))
                    if u >= CCH:
                        for l in range(LV + 1):
                            for d in range(2):
                                c = order[d][u]
                                if l < LV:
                                    S["dve"].wait(pe, ("kl", u, l, d), i)
                                if l:
                                    S["dve"].wait(pe, ("pm", u, l - 1, d), i)
                                elif u > CCH:
                                    S["dve"].wait(pe, ("o", u - 1, d), i)
                                for hh in range(2):
                                    lo, ro = ((GU["kl"][:, d, hh, :], GU["ql"][:, d, hh, :]) if l < LV else
                                              (gk[:, hh, cs(c)], gq[:, hh, cs(c)]))
                                    mm = pe.matmul(ps[:, 5 + 2 * d, cs(hh)], lhsT=lo, rhs=ro, start=True, stop=True)
                                me.done(mm, ("P", u, l, d))
                        for d in range(2):
                            c = order[d][u]
                            S["dve"].wait(pe, ("ac", u, LV, d), i)
                            for n in range(4):
                                hh, vt = n // 2, n % 2
                                pe.matmul(ps[:, 5 + 2 * d, cs(n)], lhsT=gS[:, d, hh, vt * P:(vt + 1) * P],
                                          rhs=GU["qe"][:, d, hh, :], start=True, stop=False)
                                mm = pe.matmul(ps[:, 5 + 2 * d, cs(n)], lhsT=gv[:, c, n * P:(n + 1) * P],
                                               rhs=GU["at"][:, d, hh, :], start=False, stop=True)
                            me.done(mm, ("O", u, d))
                    for d in range(2):
                        c = order[d][u]
                        S["act"].wait(pe, ("tkc", u, d), i)
                        for hh in range(2):
                            mm = pe.matmul(ps[:, 4 + 2 * d, 256 * hh:256 * hh + 256], lhsT=GU["ktm"][:, d, hh, :],
                                           rhs=gv[:, c, 256 * hh:256 * hh + 256], start=True, stop=True)
                        me.done(mm, ("DS", u, d))
                for d in range(2):
                    S["dve"].wait(pe, ("s", NCH - 1, d), i)
                for n in range(2):
                    for m in range(2):
                        S["act"].wait(pe, ("sq", 2 * n + m), i)
                        mm = pe.matmul(ps[:, 5 + 2 * n, 0:NX], lhsT=ones[:, :], rhs=sqb[:, m, NC_:T],
                                       start=(m == 0), stop=(m == 1))
                    me.done(mm, ("ss", n))
                up_slab(pe, s + 2, t + 10, h, i=i, sper=4, tper=22, ctxt=False)
                S["dve"].wait(pe, ("oz", 3), i)
                down_slab(pe, s + 3, t + 14, lambda k: go[:, k, :], i=i, sper=4, tper=22, ctxt=False)

        def gla_act(act):
            t = at["gla"][1]
            act.wait_ge(gp, 1)
            for d in range(2):
                act.activation(glow[0:16, d, 0:NC_], ps[0:16, 4 + 2 * d, 0:NC_], ACT.Copy)
                x_ = act.activation(glow[0:16, d, NC_:T], ps[0:16, 5 + 2 * d, 0:NX], ACT.Copy)
            x_.then_inc(gpa, 1)
            S = gSt
            me = S["act"]
            me.start(act)
            with act.Fori(0, 2) as i:
                others(act, S, "act", i)
                act.wait_ge(me.sem, i * len(me.steps) + 1)
                for n in range(4):
                    tile_wait(act, t + n, i, 22)
                    dst, sc = (gq[:, n, :], float(P) ** -0.5) if n < 2 else (gk[:, n - 2, :], 1.0)
                    act.activation(dst[:, 0:NC_], bank(t + n, 0)[:, 0:NC_], ACT.Copy, scale=sc)
                    act.activation(dst[:, NC_:T], bank(t + n, 1)[:, 0:NX], ACT.Copy, scale=sc)\
                        .then_inc(pair_free[(t + n) % 2], 1)
                for n in range(6):
                    tile_wait(act, t + 4 + n, i, 22)
                    act.activation(gv[:, n, :], bank(t + 4 + n, 1), ACT.Copy).then_inc(pair_free[(t + n) % 2], 1)
                act.preload_act_table_set("natural_log_exp_and_others")
                for n in range(4):
                    S["dve"].wait(act, ("na", n), i)
                    me.done(act.activation(gx[:, 1, :], gx[:, 1, :], ACT.Exp), ("e1", n))
                    mine(S, "act", act, i)
                    me.done(act.activation(gx[:, 1, :], gx[:, 1, :], ACT.Ln, bias=1.0), ("l1", n))
                for u in range(NCH):
                    for d in range(2):
                        c = order[d][u]
                        S["dve"].wait(act, ("tl", u, d), i)
                        me.done(act.activation(GU["e"][:, d, :, :], GU["e"][:, d, :, :], ACT.Exp, scale=-1 / 16.),
                                ("te", u, d))
                        me.done(act.activation(GU["eb"][:, d, :, :], gB[:, 2 * d:2 * d + 2, cs(c)], ACT.Exp,
                                               scale=1 / 16.), ("eb", u, d))
                        S["pe"].wait(act, ("TK", u, d), i)
                        me.done(act.activation(GU["ktm"][:, d, :, :].rearrange("p h n -> p (h n)"),
                                               ps[:, 4 + 2 * d, 0:256], ACT.Copy), ("tkc", u, d))
                    if u >= CCH:
                        for l in range(LV):
                            for d in range(2):
                                S["dve"].wait(act, ("ab", u, l, d), i)
                                me.done(act.activation(GU["df"][:, d, :, :], GU["df"][:, d, :, :], ACT.Exp,
                                                       scale=1 / 16.), ("ex", u, l, d))
                for n in range(2):
                    for d in range(2):
                        S["dve"].wait(act, ("o", NCH - 1, d), i)
                    if n:
                        S["pe"].wait(act, ("ss", 0), i)
                    for m in range(2):
                        me.done(act.activation(sqb[:, m, NC_:T], go[:, 2 * n + m, NC_:T], ACT.Square),
                                ("sq", 2 * n + m))
                    S["pe"].wait(act, ("ss", n), i)
                    if n:
                        S["dve"].wait(act, ("on", 1), i)
                    me.done(act.activation(rnb[:, NC_:T], ps[:, 5 + 2 * n, 0:NX], ACT.Ln, bias=epsc[:, 0:1],
                                           scale=1.0 / 256), ("ln", n))
                    mine(S, "act", act, i)
                    me.done(act.activation(rnb[:, NC_:T], rnb[:, NC_:T], ACT.Exp, scale=-0.5), ("rn", n))
                for n in range(4):
                    tile_wait(act, t + 10 + n, i, 22)
                    if n >= 2:
                        S["dve"].wait(act, ("oz", n - 2), i)
                    act.activation(gzb[:, n % 2, NC_:T], bank(t + 10 + n, 1)[:, 0:NX], ACT.Silu)\
                        .then_inc(pair_free[(t + n) % 2], 1)

        def gla_dve(dve):
            t = at["gla"][1]
            v = dve
            S = gSt
            me = S["dve"]
            me.start(v)

            def do_(ins, step):
                me.done(ins, step)

            with dve.Fori(0, 2) as i:
                others(v, S, "dve", i)
                v.wait_ge(gin, 48)
                mine(S, "dve", v, i)
                v.tensor_copy(gw2c[0:16, :, :], gw2[0:16, :, bass.ds(i * 256, 256)])
                do_(v.tensor_copy(gb2c[:, :, :], gb2[:, :, bass.ds(i * 2, 2)]), "cur")
                for n in range(4):
                    d, hh, b = n // 2, n % 2, 4 + 2 * (n % 2)
                    S["pe"].wait(v, ("lg", n), i)
                    mine(S, "dve", v, i)
                    v.tensor_scalar(gx[:, 0, 0:NC_], ps[:, b, 0:NC_], gb2c[:, d, hh:hh + 1], None, ALU.add)
                    do_(v.tensor_scalar(gx[:, 0, NC_:T], ps[:, b + 1, 0:NX], gb2c[:, d, hh:hh + 1], None,
                                        ALU.add), ("x", n))
                    mine(S, "dve", v, i)
                    do_(v.scalar_tensor_tensor(out=gx[:, 1, :], in0=gx[:, 0, :], scalar=-1.0, in1=gx[:, 0, :],
                                               op0=ALU.mult, op1=ALU.min), ("na", n))
                    S["act"].wait(v, ("l1", n), i)
                    do_(v.scalar_tensor_tensor(out=gx[:, 0, :], in0=gx[:, 0, :], scalar=0.0, in1=gx[:, 1, :],
                                               op0=ALU.min, op1=ALU.subtract), ("t", n))
                    mine(S, "dve", v, i)
                    if d == 0:
                        ins = v.tensor_tensor_scan(gB[:, n, :], rst[:, :], gx[:, 0, :], 0.0, ALU.mult, ALU.add)
                    else:
                        ins = v.tensor_tensor_scan(gB[:, n, T - 1::-1], rst[:, :], gx[:, 0, T - 1::-1], 0.0,
                                                   ALU.mult, ALU.add)
                    do_(ins, ("sc", n))
                for n in range(2):
                    v.wait_ge(pair_free[(t + n) % 2], lin(i, (t + 8 + n) // 2 + 1, 11))
                v.memset(go, 0.0)
                do_(v.memset(gS, 0.0), "s0")
                for u in range(NCH):
                    for d in range(2):
                        c = order[d][u]
                        e = c * P + (P - 1 if d == 0 else 0)
                        mine(S, "dve", v, i)
                        do_(v.tensor_tensor(GU["e"][:, d, :, :], gB[:, 2 * d:2 * d + 2, cs(c)],
                                            gB[:, 2 * d:2 * d + 2, e:e + 1].broadcast_to([P, 2, P]),
                                            ALU.subtract), ("tl", u, d))
                    for d in range(2):
                        c = order[d][u]
                        S["act"].wait(v, ("te", u, d), i)
                        if u:
                            S["pe"].wait(v, ("TK", u - 1, d), i)
                        do_(v.tensor_tensor(GU["kt"][:, d, :, :], gk[:, :, cs(c)], GU["e"][:, d, :, :],
                                            ALU.mult), ("kt", u, d))
                    if u >= CCH:
                        for d in range(2):
                            c = order[d][u]
                            S["act"].wait(v, ("eb", u, d), i)
                            v.memset(GU["at"][:, d, :, :], 0.0)
                            do_(v.tensor_tensor(GU["qe"][:, d, :, :], gq[:, :, cs(c)], GU["eb"][:, d, :, :],
                                                ALU.mult), ("qe", u, d))
                        for l in range(LV + 1):
                            s = 1 << min(l, LV - 1)
                            for d in range(2):
                                if l == LV:
                                    continue
                                c = order[d][u]
                                for hh in range(2):
                                    bv = gB[:, 2 * d + hh, cs(c)].rearrange("p (b n) -> p b n", n=2 * s)
                                    r = s - 1 if d == 0 else s
                                    mine(S, "dve", v, i)
                                    ins = v.tensor_tensor(GU["df"][:, d, hh, :].rearrange("p (b n) -> p b n", n=2 * s),
                                                          bv, bv[:, :, r:r + 1].broadcast_to([P, P // (2 * s), 2 * s]),
                                                          ALU.subtract)
                                do_(ins, ("df", u, l, d))
                                mine(S, "dve", v, i)
                                do_(v.scalar_tensor_tensor(out=GU["df"][:, d, :, :], in0=GU["df"][:, d, :, :],
                                                           scalar=-1.0, in1=GU["df"][:, d, :, :], op0=ALU.mult,
                                                           op1=ALU.min), ("ab", u, l, d))
                            for d in range(2):
                                if l == LV:
                                    continue
                                c = order[d][u]
                                S["act"].wait(v, ("ex", u, l, d), i)
                                do_(v.tensor_tensor(GU["ql"][:, d, :, :], gq[:, :, cs(c)], GU["df"][:, d, :, :],
                                                    ALU.mult), ("ql", u, l, d))
                                do_(v.tensor_tensor(GU["kl"][:, d, :, :], gk[:, :, cs(c)], GU["df"][:, d, :, :],
                                                    ALU.mult), ("kl", u, l, d))
                            for d in range(2):
                                S["pe"].wait(v, ("P", u, l, d), i)
                                m = maskL[:, d, l, :] if l < LV else ident[:, :]
                                mine(S, "dve", v, i)
                                do_(v.tensor_tensor(GU["pm"][:, d, :, :],
                                                    ps[:, 5 + 2 * d, 0:256].rearrange("p (h n) -> p h n", h=2),
                                                    m.rearrange("p (h n) -> p h n", h=1).broadcast_to([P, 2, P]),
                                                    ALU.mult), ("pm", u, l, d))
                                mine(S, "dve", v, i)
                                do_(v.tensor_tensor(GU["at"][:, d, :, :], GU["at"][:, d, :, :],
                                                    GU["pm"][:, d, :, :], ALU.add), ("ac", u, l, d))
                        for d in range(2):
                            c = order[d][u]
                            S["pe"].wait(v, ("O", u, d), i)
                            mine(S, "dve", v, i)
                            do_(v.tensor_tensor(go[:, :, cs(c)], go[:, :, cs(c)], bk(5 + 2 * d), ALU.add),
                                ("o", u, d))
                    for d in range(2):
                        S["pe"].wait(v, ("DS", u, d), i)
                        S["act"].wait(v, ("tkc", u, d), i)
                        e = P - 1 if d == 0 else 0
                        for hh in range(2):
                            mine(S, "dve", v, i)
                            ins = v.scalar_tensor_tensor(out=gS[:, d, hh, :], in0=gS[:, d, hh, :],
                                                         scalar=GU["eb"][:, d, hh, e:e + 1],
                                                         in1=ps[:, 4 + 2 * d, 256 * hh:256 * hh + 256],
                                                         op0=ALU.mult, op1=ALU.add)
                        do_(ins, ("s", u, d))
                for n in range(2):
                    S["act"].wait(v, ("rn", n), i)
                    for m in range(2):
                        mine(S, "dve", v, i)
                        do_(v.scalar_tensor_tensor(out=go[:, 2 * n + m, NC_:T], in0=go[:, 2 * n + m, NC_:T],
                                                   scalar=gng[:, m:m + 1], in1=rnb[:, NC_:T], op0=ALU.mult,
                                                   op1=ALU.mult), ("on", 2 * n + m))
                for n in range(4):
                    v.wait_ge(pair_free[(t + n) % 2], lin(i, (t + 10 + n) // 2 + 1, 11))
                    mine(S, "dve", v, i)
                    do_(v.tensor_tensor(go[:, n, NC_:T], go[:, n, NC_:T], gzb[:, n % 2, NC_:T], ALU.mult), ("oz", n))
                for m in range(KT):
                    add_gated(v, t + 14 + m, 1, 2, m, i, 22, False)
                end_of_updates(v, t + 21, i, 11)
                mine(S, "dve", v, i)
                do_(v.memset(scr[:, 0:1], 0.0), "end")
            me.passes(v, 2)
            v.memset(scr[:, 1:2], 0.0).then_inc(resid_ready, 1)

        def gla_pool(pool):
            h_wait(pool, "nm1")
            for dst, src in ((gwl, a["gla_w_in"][:, 3072:3104].rearrange("(k p) n -> p k n", p=P)),
                             (gw2[0:16, :, :], a["gw2"]), (rst[:, :], a["rst"])):
                pool.dma_start(dst, src).then_inc(gin, 16)

        GLA = (gla_pe, gla_act, gla_dve, gla_pool) if "gla" in MIX else None
        mq = arena(22 * T, 4, T)
        mk = arena(0, 2, T)
        mv = arena(2 * T, NCH, 512)
        mo = arena(6 * T, 4, T)
        mkt = arena(10 * T, NCH, 256)
        mr = arena(12 * T, 2, 5, T)
        off = 26 * T
        MU = {}
        for nm in ["tmp", "wt", "qc", "kw", "hd"]:
            MU[nm] = arena(off, 2, 4, P)
            off += 1024
        mraw = arena(off - 2048, T)
        mrst = arena(off - 1024, T)
        mwg = arena(off - 3072, KT, 32)
        mzb = arena(26 * T, 2, T)
        mac = arena(26 * T + 5120, 2, 2, NCH, 8)
        macc = arena(26 * T + 5312, 2, 2, NCH, 4)
        msel = sb("msel", [8, 4])
        mhn = sb("mhn", [P, 8])
        mhnc = sb("mhnc", [P, 4])
        mgb = sb("mgb", [32, 1])
        mdec = sb("mdec", [P, 2, 4])
        min_, mpp, mpv, mpa = (sem("mlstm_" + n) for n in ("weights_in", "prep_pe", "prep_dve", "prep_act"))
        MPV = [0]

        def msteps():
            pe, act, dve = [], [], ["cur"]
            for n in range(3):
                pe.append(("tr", n))
                act.append(("trc", n))
            dve.append("s0")
            for u in range(NCH):
                for d in range(2):
                    pe += [("R", u, d), ("K", u, d)]
                    dve += [("a1", u, d), ("a2", u, d), ("kw", u, d)]
                    act.append(("ex", u, d))
                    pe.append(("C", u, d))
                for d in range(2):
                    dve += [("wt", u, d), ("qc", u, d)]
                    pe += [("N", u, d), ("D", u, d)]
                    act.append(("ab", u, d))
                    pe.append(("E", u, d))
                for d in range(2):
                    dve += [("mx", u, d), ("rc", u, d), ("nm", u, d), ("o", u, d)]
                    pe.append(("DS", u, d))
                for d in range(2):
                    dve.append(("s", u, d))
            for n in range(4):
                act += [("osq", n), ("oln", n), ("orn", n)]
                pe.append(("oss", n))
                dve.append(("on", n))
            dve += [("oz", n) for n in range(4)] + ["end"]
            return pe, act, dve

        mS = dict(zip(["pe", "act", "dve"], [Steps("mlstm_" + n, s) for n, s in zip(["pe", "act", "dve"], msteps())]))

        def pr(hh):
            return slice(64 * (hh % 2), 64 * (hh % 2) + 64)

        def ml_pe(pe):
            s, t = at["ml"]
            h_wait(pe, "nm2")
            pe.wait_ge(min_, 32)
            for (b, c0, n) in ((4, 0, NC_), (5, NC_, NX)):
                for k in range(KT):
                    mm = pe.matmul(ps[0:32, b, 0:n], lhsT=mwg[:, k, :], rhs=h[:, k, c0:c0 + n],
                                   start=(k == 0), stop=(k == KT - 1))
            mm.then_inc(mpp, 1)
            pe.wait_ge(mpv, 1)
            for n in range(4):
                if n >= 2:
                    pe.wait_ge(mpa, n - 1)
                for (b, c0, w) in ((4, 0, NC_), (5, NC_, NX)):
                    mm = pe.matmul(ps[0:8, b + 2 * (n % 2), 0:w], lhsT=ident[0:32, 8 * n:8 * n + 8],
                                   rhs=mraw[0:32, c0:c0 + w], start=True, stop=True)
                mm.then_inc(mpp, 1)
            pe.wait_ge(mpv, MPREP)
            pe.wait_ge(mpa, 9)
            for kk, kind in enumerate((0, 4)):
                for d in range(2):
                    for c in range(NCH):
                        o = 8 * (c + NCH * (d + 2 * kk))
                        mm = pe.transpose(ps[:, 4, o:o + 8], mr[0:8, d, kind, cs(c)], ident[0:8, 0:8])
            mm.then_inc(mpp, 1)
            pe.wait_ge(mpa, 10)
            S = mS
            me = S["pe"]
            me.start(pe)
            with pe.Fori(0, 2) as i:
                others(pe, S, "pe", i)
                up_slab(pe, s, t, h, i=i, sper=4, tper=22)
                v_tiles(pe, s + 1, t + 4, i, 4, 22)
                for n in range(2):
                    pe.wait_ge(pair_free[(t + n) % 2], lin(i, (t + 8 + n) // 2 + 1, 11))
                for n in range(3):
                    for m in range(4):
                        mm = pe.transpose(ps[:, 4 + n, cs(m)], mk[:, m % 2, cs(2 * n + m // 2)], ident[:, :])
                    me.done(mm, ("tr", n))
                S["dve"].wait(pe, "s0", i)

                def rows(b, d, kind, c):
                    for hh in range(4):
                        mm = pe.matmul(ps[:, b, cs(hh)], lhsT=msel[0:8, hh:hh + 1].broadcast_to([8, P]),
                                       rhs=mr[0:8, d, kind, cs(c)], start=True, stop=True)
                    return mm

                for u in range(NCH):
                    for d in range(2):
                        c = order[d][u]
                        if u:
                            S["dve"].wait(pe, ("s", u - 1, d), i)
                        else:
                            S["act"].wait(pe, ("trc", 2), i)
                        me.done(rows(4 + 2 * d, d, 2, c), ("R", u, d))
                        for hh in range(4):
                            mm = pe.matmul(ps[:, 5 + 2 * d, cs(hh)], lhsT=mk[:, hh // 2, cs(c)],
                                           rhs=mq[:, hh, cs(c)], start=True, stop=True)
                        me.done(mm, ("K", u, d))
                        S["dve"].wait(pe, ("a1", u, d), i)
                        me.done(rows(4 + 2 * d, d, 1, c), ("C", u, d))
                    for d in range(2):
                        c = order[d][u]
                        S["dve"].wait(pe, ("qc", u, d), i)
                        for which in range(2):
                            for hh in range(4):
                                o = ps[:, (5 if which == 0 else 4) + 2 * d, cs(hh)]
                                pe.matmul(o, lhsT=US[:, d, 2 * (hh // 2) + which, :],
                                          rhs=MU["qc"][:, d, hh, :], start=True, stop=False)
                                mm = pe.matmul(o, lhsT=mv[:, c, cs(hh)] if which == 0 else ones[:, :],
                                               rhs=MU["wt"][:, d, hh, :], start=False, stop=True)
                            me.done(mm, ("ND"[which], u, d))
                        S["act"].wait(pe, ("ab", u, d), i)
                        me.done(rows(4 + 2 * d, d, 3, c), ("E", u, d))
                    for d in range(2):
                        c = order[d][u]
                        S["dve"].wait(pe, ("nm", u, d), i)
                        for hh in range(4):
                            for which in range(2):
                                mm = pe.matmul(ps[pr(hh), 5 + 2 * d, cs(2 * (hh // 2) + which)],
                                               lhsT=MU["kw"][:, d, hh // 2, 64 * (hh % 2):64 * (hh % 2) + 64],
                                               rhs=mv[:, c, cs(hh)] if which == 0 else ones[:, :],
                                               start=True, stop=True)
                        me.done(mm, ("DS", u, d))
                for n in range(4):
                    S["act"].wait(pe, ("osq", n), i)
                    b = 4 + 2 * (n % 2)
                    if n == 0:
                        for d in range(2):
                            S["dve"].wait(pe, ("s", NCH - 1, d), i)
                    if n >= 2:
                        S["act"].wait(pe, ("oln", n - 2), i)
                    pe.matmul(ps[:, b, 0:NC_], lhsT=ones[:, :], rhs=sqb[:, n % 2, 0:NC_], start=True, stop=True)
                    me.done(pe.matmul(ps[:, b + 1, 0:NX], lhsT=ones[:, :], rhs=sqb[:, n % 2, NC_:T],
                                      start=True, stop=True), ("oss", n))
                up_slab(pe, s + 2, t + 10, h, i=i, sper=4, tper=22)
                S["dve"].wait(pe, ("oz", 3), i)
                down_slab(pe, s + 3, t + 14, lambda k: mo[:, k, :], i=i, sper=4, tper=22)

        def ml_act(act):
            t = at["ml"][1]
            for n in range(4):
                act.wait_ge(mpp, n + 2)
                for (b, c0, w) in ((4, 0, NC_), (5, NC_, NX)):
                    ins = act.activation(mr[0:8, n // 2, n % 2, c0:c0 + w], ps[0:8, b + 2 * (n % 2), 0:w], ACT.Copy)
                ins.then_inc(mpa, 1)
            act.wait_ge(mpv, 2)
            act.activation(mr[0:8, :, 2, :], mr[0:8, :, 2, :], ACT.Exp).then_inc(mpa, 1)
            act.wait_ge(mpa, 5)
            act.activation(mr[0:8, :, 2, :], mr[0:8, :, 2, :], ACT.Ln, bias=1.0).then_inc(mpa, 1)
            act.wait_ge(mpv, MPREP)
            act.activation(mr[0:8, :, 1, :], mr[0:8, :, 1, :], ACT.Exp).then_inc(mpa, 1)
            act.activation(mr[0:8, :, 4, :], mr[0:8, :, 4, :], ACT.Exp).then_inc(mpa, 1)
            act.activation(mr[0:8, :, 3, :], mr[0:8, :, 3, :], ACT.Exp, scale=-1.0).then_inc(mpa, 1)
            act.wait_ge(mpp, 6)
            act.activation(mac[:, :, :, :, :].rearrange("p a b c d -> p (a b c d)"), ps[:, 4, 0:192], ACT.Copy)\
                .then_inc(mpa, 1)
            S = mS
            me = S["act"]
            me.start(act)
            with act.Fori(0, 2) as i:
                others(act, S, "act", i)
                for n in range(4):
                    tile_wait(act, t + n, i, 22)
                    if n < 2:
                        for hh in (2 * n, 2 * n + 1):
                            act.activation(mq[pr(hh), hh, 0:NC_], bank(t + n, 0)[pr(hh), 0:NC_], ACT.Copy)
                            ins = act.activation(mq[pr(hh), hh, NC_:T], bank(t + n, 1)[pr(hh), 0:NX], ACT.Copy)
                        ins.then_inc(pair_free[(t + n) % 2], 1)
                        continue
                    dst, sc = mk[:, n - 2, :], 0.125
                    act.activation(dst[:, 0:NC_], bank(t + n, 0)[:, 0:NC_], ACT.Copy, scale=sc)
                    act.activation(dst[:, NC_:T], bank(t + n, 1)[:, 0:NX], ACT.Copy, scale=sc)\
                        .then_inc(pair_free[(t + n) % 2], 1)
                for n in range(6):
                    tile_wait(act, t + 4 + n, i, 22)
                    act.activation(mv[:, n, :], bank(t + 4 + n, 1), ACT.Copy).then_inc(pair_free[(t + n) % 2], 1)
                act.preload_act_table_set("natural_log_exp_and_others")
                for n in range(3):
                    S["pe"].wait(act, ("tr", n), i)
                    me.done(act.activation(mkt[:, 2 * n:2 * n + 2, :].rearrange("p c n -> p (c n)"),
                                           ps[:, 4 + n, :], ACT.Copy), ("trc", n))
                for u in range(NCH):
                    for d in range(2):
                        S["dve"].wait(act, ("a2", u, d), i)
                        me.done(act.activation(MU["wt"][:, d, :, :], MU["tmp"][:, d, :, :], ACT.Exp), ("ex", u, d))
                    for d in range(2):
                        S["pe"].wait(act, ("D", u, d), i)
                        me.done(act.activation(MU["hd"][:, d, :, :], bk(4 + 2 * d), ACT.Abs), ("ab", u, d))
                for n in range(4):
                    me_norm(act, S, i, n, mo[:, n, :], ("osq", n), ("oss", n), ("oln", n), ("orn", n), 1.0 / P,
                            [], ("on", n - 1) if n else None, [("s", NCH - 1, 0), ("o", NCH - 1, 1)])
                for n in range(4):
                    tile_wait(act, t + 10 + n, i, 22)
                    if n >= 2:
                        S["dve"].wait(act, ("oz", n - 2), i)
                    act.activation(mzb[:, n % 2, 0:NC_], bank(t + 10 + n, 0)[:, 0:NC_], ACT.Sigmoid)
                    act.activation(mzb[:, n % 2, NC_:T], bank(t + 10 + n, 1)[:, 0:NX], ACT.Sigmoid)\
                        .then_inc(pair_free[(t + n) % 2], 1)

        def ml_prep_ops():
            al, ca, be, em, w = range(5)
            ops = []
            R8 = lambda d, k: mr[0:8, d, k, :]
            LAST = [P - 1, 0]
            ops.append(lambda v: v.scalar_tensor_tensor(out=mr[0:8, :, 4, :], in0=mr[0:8, :, 1, :], scalar=0.0,
                                                        in1=mr[0:8, :, 2, :], op0=ALU.min, op1=ALU.subtract))
            for d in range(2):
                r = slice(None) if d == 0 else slice(T - 1, None, -1)
                ops.append(lambda v, d=d, r=r: v.tensor_tensor_scan(mr[0:8, d, 2, r], mrst[0:8, :], mr[0:8, d, 4, r],
                                                                    0.0, ALU.mult, ALU.add))
            ops.append(lambda v: v.tensor_tensor_scan(mr[0:8, 0, 3, :], mr[0:8, 0, 4, :], mr[0:8, 0, 0, :],
                                                      0.0, ALU.add, ALU.max))
            rc, rx = slice(NC_ - 1, None, -1), slice(T - 1, NC_ - 1, -1)
            ops.append(lambda v: v.tensor_tensor_scan(mr[0:8, 1, 3, rc], mr[0:8, 1, 4, rc], mr[0:8, 1, 0, rc],
                                                      0.0, ALU.add, ALU.max))
            ops.append(lambda v: v.tensor_tensor_scan(mr[0:8, 1, 3, rx], mr[0:8, 1, 4, rx], mr[0:8, 1, 0, rx],
                                                      mr[0:8, 1, 3, 0:1], ALU.add, ALU.max))
            ops.append(lambda v: v.tensor_tensor(mr[0:8, :, 0, :], mr[0:8, :, 0, :], mr[0:8, :, 2, :], ALU.subtract))
            ops.append(lambda v: v.tensor_tensor(mr[0:8, :, 2, :], mr[0:8, :, 2, :], mr[0:8, :, 3, :], ALU.subtract))
            for d in range(2):
                for u, c in enumerate(order[d]):
                    if u == 0:
                        m0 = 0.0
                    else:
                        pc = order[d][u - 1] * P + LAST[d]
                        m0 = mr[0:8, d, 3, pc:pc + 1]
                    e = c * P + LAST[d]
                    ops.append(lambda v, d=d, c=c, m0=m0: v.tensor_scalar(mr[0:8, d, 1, cs(c)], mr[0:8, d, 2, cs(c)],
                                                                          m0, None, ALU.add))
                    ops.append(lambda v, d=d, c=c, e=e: v.tensor_scalar(mr[0:8, d, 4, cs(c)], mr[0:8, d, 0, cs(c)],
                                                                        mr[0:8, d, 2, e:e + 1], None, ALU.add))
            return ops

        MPO = ml_prep_ops()
        MPREP = 2 + len(MPO)

        def ml_dve(dve):
            t = at["ml"][1]
            v = dve
            S = mS
            me = S["dve"]
            me.start(v)
            v.wait_ge(mpp, 1)
            v.memset(mq, 0.0)
            v.tensor_scalar(mraw[0:32, 0:NC_], ps[0:32, 4, 0:NC_], mgb[:, 0:1], None, ALU.add)
            v.tensor_scalar(mraw[0:32, NC_:T], ps[0:32, 5, 0:NX], mgb[:, 0:1], None, ALU.add).then_inc(mpv, 1)
            v.wait_ge(mpa, 4)
            v.scalar_tensor_tensor(out=mr[0:8, :, 2, :], in0=mr[0:8, :, 1, :], scalar=-1.0, in1=mr[0:8, :, 1, :],
                                   op0=ALU.mult, op1=ALU.min).then_inc(mpv, 1)
            v.wait_ge(mpa, 6)
            v.wait_ge(min_, 32)
            for n, op in enumerate(MPO):
                v.wait_ge(mpv, 2 + n)
                op(v).then_inc(mpv, 1)
            v.wait_ge(mpa, 10)

            def do_(ins, step):
                me.done(ins, step)

            with dve.Fori(0, 2) as i:
                others(v, S, "dve", i)
                mine(S, "dve", v, i)
                v.tensor_copy(macc[:, :, :, :, :].rearrange("p a b c d -> p (a b c) d"),
                              mac[:, :, :, :, :].rearrange("p a b c d -> p (a b c) d")[:, :, bass.ds(i * 4, 4)])
                v.tensor_copy(mhnc[:, :], mhn[:, bass.ds(i * 4, 4)])
                do_(v.tensor_copy(msel[0:8, :], ident[0:8, bass.ds(i * 4, 4)]), "cur")
                v.memset(mo, 0.0)
                do_(v.memset(US[:, :, :, :], 0.0), "s0")
                S["act"].wait(v, ("trc", 2), i)
                for u in range(NCH):
                    for d in range(2):
                        c = order[d][u]
                        S["pe"].wait(v, ("R", u, d), i)
                        mine(S, "dve", v, i)
                        do_(v.tensor_tensor(MU["tmp"][:, d, :, :], bk(4 + 2 * d), four(macc[:, 0, d, c, :]),
                                            ALU.add), ("a1", u, d))
                        mine(S, "dve", v, i)
                        do_(v.tensor_tensor(MU["tmp"][:, d, :, :], MU["tmp"][:, d, :, :], spread(negm[:, d, :]),
                                            ALU.add), ("a2", u, d))
                        do_(v.tensor_tensor(MU["kw"][:, d, 0:2, :].rearrange("p t (g n) -> p (t g) n", g=2),
                                            mkt[:, c, :].rearrange("p (h n) -> p h n", h=4),
                                            macc[:, 1, d, c, :].rearrange("p (h n) -> p h n", n=1)
                                            .broadcast_to([P, 4, 64]), ALU.mult), ("kw", u, d))
                    for d in range(2):
                        c = order[d][u]
                        e = P - 1 if d == 0 else 0
                        S["act"].wait(v, ("ex", u, d), i)
                        S["pe"].wait(v, ("C", u, d), i)
                        do_(v.tensor_tensor(MU["wt"][:, d, :, :], MU["wt"][:, d, :, :], bk(5 + 2 * d), ALU.mult),
                            ("wt", u, d))
                        v.tensor_copy(mdec[:, d, :].rearrange("p (h n) -> p h n", n=1), bk(4 + 2 * d)[:, :, e:e + 1])
                        ins = v.tensor_tensor(MU["qc"][:, d, :, :], mq[:, :, cs(c)], bk(4 + 2 * d), ALU.mult)
                        do_(ins, ("qc", u, d))
                    for d in range(2):
                        c = order[d][u]
                        S["pe"].wait(v, ("E", u, d), i)
                        hd = MU["hd"][:, d, :, :]
                        do_(v.tensor_tensor(hd, hd, bk(4 + 2 * d), ALU.max), ("mx", u, d))
                        mine(S, "dve", v, i)
                        do_(v.reciprocal(hd, hd), ("rc", u, d))
                        mine(S, "dve", v, i)
                        do_(v.tensor_tensor(hd, hd, bk(5 + 2 * d), ALU.mult), ("nm", u, d))
                        mine(S, "dve", v, i)
                        do_(v.tensor_tensor(mo[:, :, cs(c)], mo[:, :, cs(c)], hd, ALU.add), ("o", u, d))
                    for d in range(2):
                        S["pe"].wait(v, ("DS", u, d), i)
                        for hh in range(4):
                            q2 = slice(2 * (hh // 2), 2 * (hh // 2) + 2)
                            ins = v.scalar_tensor_tensor(out=US[pr(hh), d, q2, :], in0=US[pr(hh), d, q2, :],
                                                         scalar=mdec[pr(hh), d, hh:hh + 1],
                                                         in1=bk(5 + 2 * d)[pr(hh), q2, :], op0=ALU.mult, op1=ALU.add)
                        do_(ins, ("s", u, d))
                for n in range(4):
                    S["act"].wait(v, ("orn", n), i)
                    mine(S, "dve", v, i)
                    do_(v.scalar_tensor_tensor(out=mo[:, n, :], in0=mo[:, n, :], scalar=mhnc[:, n:n + 1],
                                               in1=rnb[:, :], op0=ALU.mult, op1=ALU.mult), ("on", n))
                for n in range(4):
                    v.wait_ge(pair_free[(t + n) % 2], lin(i, (t + 10 + n) // 2 + 1, 11))
                    mine(S, "dve", v, i)
                    do_(v.tensor_tensor(mo[:, n, :], mo[:, n, :], mzb[:, n % 2, :], ALU.mult), ("oz", n))
                for m in range(KT):
                    add_gated(v, t + 14 + m, 2, 2, m, i, 22)
                end_of_updates(v, t + 21, i, 11)
                mine(S, "dve", v, i)
                do_(v.memset(scr[:, 0:1], 0.0), "end")
            me.passes(v, 2)
            v.memset(scr[:, 1:2], 0.0).then_inc(resid_ready, 1)

        def ml_pool(pool):
            h_wait(pool, "nm2")
            for dst, src in ((mwg, a["mlstm_w_in"][:, 3072:3104].rearrange("(k p) n -> p k n", p=P)),
                             (mrst[:, :], a["rst"])):
                pool.dma_start(dst, src).then_inc(min_, 16)

        ML = (ml_pe, ml_act, ml_dve, ml_pool) if "ml" in MIX else None
        wq_ = arena(0, 8, NX)
        kz = arena(4096, 4, 2, T)
        wv = arena(4096 + 8 * T, NCH, 256)
        wo_ = arena(4096 + 10 * T, 8, T)
        kd = arena(4096 + 10 * T, 4, T)
        rtab = arena(4096 + 18 * T, 2, NX)
        rotm = arena(5120 + 18 * T, P)
        off = 5120 + 18 * T + P
        wp = arena(off, 2, 640)
        wpt = arena(off + 1280, 2, 640)
        rtmp = arena(off + 1280, 2, NX)
        sinkc = sb("sinkc", [P, 16])
        sst = sb("sst", [P, 2, 6])
        swin = sem("swa_tables_in")
        swk = sem("swa_kz")
        UN = [(hh, b) for hh in range(16) for b in range(4)]

        def ssteps():
            pe, act, dve = [], [], []
            for n in range(12):
                pe.append(("rot", n))
                dve += [("cos", n), ("sin", n), ("add", n)]
            dve.append("kz")
            for u in range(len(UN) + 1):
                if u:
                    dve += [("den", u - 1), ("rec", u - 1), ("pn", u - 1)]
                    act.append(("tc", u - 1))
                if u < len(UN):
                    pe.append(("S", u))
                    dve += [("sc", u), ("mx", u), ("ms", u), ("nm", u)]
                    act += [("e", u), ("es", u)]
                if u:
                    pe += [("T", u - 1), ("O", u - 1)]
                    dve.append(("o", u - 1))
            return pe, act, dve

        sS = dict(zip(["pe", "act", "dve"], [Steps("swa_" + n, s) for n, s in zip(["pe", "act", "dve"], ssteps())]))

        def keys(b):
            lo, hi = max(b - 1, 0), min(b + 1, 3)
            return lo, hi, (hi - lo + 1) * P

        def rtile(n):
            return wq_[:, n, :] if n < 8 else kd[:, n - 8, NC_:T]

        def swa_pe(pe):
            s, t = at["swa"]
            h_wait(pe, "nm3")
            for q in range(2):
                up_slab(pe, s + q, t + 4 * q, h, ctxt=False)
            slab_wait(pe, s + 2)
            w = wslab(s + 2, KT, 512)
            for g in range(4):
                product_tile(pe, t + 8 + g, KT,
                             lambda k: w[:, k, cs(g)], lambda k: h[:, k, :])
            slab_wait(pe, s + 3)
            w2 = wslab(s + 3, KT, 256)
            for c in range(NCH):
                pair_wait(pe, t + 12 + c)
                for k in range(KT):
                    mm = pe.matmul(bank(t + 12 + c, 1)[:, 0:256], lhsT=h[:, k, cs(c)], rhs=w2[:, k, :],
                                   start=(k == 0), stop=(k == KT - 1))
                mm.then_inc(tile_ready, 1)
            S = sS
            me = S["pe"]
            me.start(pe)
            pe.wait_ge(swin, 32)
            end_of_updates(pe, t + 17)
            for n in range(12):
                if n >= 2:
                    S["dve"].wait(pe, ("sin", n - 2))
                me.done(pe.matmul(ps[:, 4 + n % 2, :], lhsT=rotm, rhs=rtile(n), start=True, stop=True), ("rot", n))
            S["dve"].wait(pe, "kz")
            for u in range(len(UN) + 1):
                if u < len(UN):
                    hh, b = UN[u]
                    p = u % 2
                    lo, hi, n = keys(b)
                    if u >= 2:
                        S["dve"].wait(pe, ("sc", u - 2))
                    q = wq_[:, hh // 2, cs(b)]
                    kk = kz[:, hh // 4, hh % 2, :]
                    pe.matmul(ps[:, 2 * p, 0:n], lhsT=q, rhs=kk[:, NC_ + lo * P:NC_ + lo * P + n],
                              start=True, stop=True)
                    me.done(pe.matmul(ps[:, 2 * p + 1, 0:NC_], lhsT=q, rhs=kk[:, 0:NC_], start=True, stop=True),
                            ("S", u))
                if u:
                    hh, b = UN[u - 1]
                    p = (u - 1) % 2
                    lo, hi, n = keys(b)
                    S["dve"].wait(pe, ("pn", u - 1))
                    if u >= 3:
                        S["dve"].wait(pe, ("o", u - 3))
                    nb = n // P + 2
                    for m in range(nb):
                        mm = pe.transpose(ps[:, 4 + 2 * p + m // 4, cs(m % 4)], wp[:, p, cs(m)], ident[:, :])
                    me.done(mm, ("T", u - 1))
                    S["act"].wait(pe, ("tc", u - 1))
                    for m in range(nb):
                        c = CCH + lo + m if m < nb - 2 else m - (nb - 2)
                        mm = pe.matmul(ps[pr(hh), 5 + 2 * p, 256:384], lhsT=wv[:, c, 64 * (hh // 4):64 * (hh // 4) + 64],
                                       rhs=wpt[:, p, cs(m)], start=(m == 0), stop=(m == nb - 1))
                    me.done(mm, ("O", u - 1))
            S["dve"].wait(pe, ("o", len(UN) - 1))
            for q in range(2):
                down_slab(pe, s + 4 + q, t + 18 + 8 * q, lambda k: wo_[:, 4 * q + k, :], ctxt=False)

        def swa_act(act):
            t = at["swa"][1]
            for n in range(8):
                tile_wait(act, t + n)
                act.activation(wq_[:, n, :], bank(t + n, 1), ACT.Copy).then_inc(pair_free[(t + n) % 2], 1)
            for g in range(4):
                tile_wait(act, t + 8 + g)
                act.activation(kd[:, g, 0:NC_], bank(t + 8 + g, 0)[:, 0:NC_], ACT.Copy)
                act.activation(kd[:, g, NC_:T], bank(t + 8 + g, 1), ACT.Copy).then_inc(pair_free[(t + g) % 2], 1)
            for c in range(NCH):
                tile_wait(act, t + 12 + c)
                act.activation(wv[:, c, :], bank(t + 12 + c, 1)[:, 0:256], ACT.Copy)\
                    .then_inc(pair_free[(t + c) % 2], 1)
            S = sS
            me = S["act"]
            me.start(act)
            for u in range(len(UN) + 1):
                if u:
                    p = (u - 1) % 2
                    n = keys(UN[u - 1][1])[2] + NC_
                    S["pe"].wait(act, ("T", u - 1))
                    act.activation(wpt[:, p, 0:min(n, 512)], ps[:, 4 + 2 * p, 0:min(n, 512)], ACT.Copy) \
                        if n > 512 else None
                    a0 = 512 if n > 512 else 0
                    me.done(act.activation(wpt[:, p, a0:n], ps[:, 4 + 2 * p + (n > 512), 0:n - a0], ACT.Copy),
                            ("tc", u - 1))
                if u < len(UN):
                    hh, b = UN[u]
                    p = u % 2
                    n = keys(b)[2] + NC_
                    S["dve"].wait(act, ("nm", u))
                    me.done(act.activation(wp[:, p, 0:n], wp[:, p, 0:n], ACT.Exp, bias=sst[:, p, 1:2],
                                           accum_out=sst[:, p, 2:3]), ("e", u))
                    me.done(act.activation(sst[:, p, 3:4], sinkc[:, hh:hh + 1], ACT.Exp, bias=sst[:, p, 1:2]),
                            ("es", u))

        def swa_dve(dve):
            t = at["swa"][1]
            v = dve
            S = sS
            me = S["dve"]
            me.start(v)
            v.wait_ge(swin, 32)
            end_of_updates(v, t + 17)
            v.memset(kz, 0.0)
            for n in range(12):
                S["pe"].wait(v, ("rot", n))
                if n:
                    mine(S, "dve", v, None)
                me.done(v.tensor_tensor(rtile(n), rtile(n), rtab[:, 0, :], ALU.mult), ("cos", n))
                me.done(v.tensor_tensor(rtmp[:, n % 2, :], ps[:, 4 + n % 2, :], rtab[:, 1, :], ALU.mult), ("sin", n))
                mine(S, "dve", v, None)
                me.done(v.tensor_tensor(rtile(n), rtile(n), rtmp[:, n % 2, :], ALU.add), ("add", n))
            mine(S, "dve", v, None)
            for g in range(4):
                for half in range(2):
                    ins = v.tensor_copy(kz[pr(half), g, half, :], kd[pr(half), g, :])
            me.done(ins, "kz")
            for u in range(len(UN) + 1):
                if u:
                    p = (u - 1) % 2
                    n = keys(UN[u - 1][1])[2] + NC_
                    S["act"].wait(v, ("es", u - 1))
                    mine(S, "dve", v, None)
                    me.done(v.tensor_tensor(sst[:, p, 4:5], sst[:, p, 2:3], sst[:, p, 3:4], ALU.add), ("den", u - 1))
                    mine(S, "dve", v, None)
                    me.done(v.reciprocal(sst[:, p, 5:6], sst[:, p, 4:5]), ("rec", u - 1))
                    mine(S, "dve", v, None)
                    me.done(v.tensor_scalar(wp[:, p, 0:n], wp[:, p, 0:n], sst[:, p, 5:6], None, ALU.mult),
                            ("pn", u - 1))
                if u < len(UN):
                    hh, b = UN[u]
                    p = u % 2
                    lo, hi, n = keys(b)
                    S["pe"].wait(v, ("S", u))
                    if u >= 2:
                        S["pe"].wait(v, ("T", u - 2))
                    mine(S, "dve", v, None)
                    for m, kb in enumerate(range(lo, hi + 1)):
                        if kb == b:
                            v.tensor_scalar(wp[:, p, cs(m)], ps[:, 2 * p, cs(m)], 0.125, None, ALU.mult)
                        else:
                            v.scalar_tensor_tensor(out=wp[:, p, cs(m)], in0=ps[:, 2 * p, cs(m)], scalar=0.125,
                                                   in1=negm[:, 0 if kb < b else 1, :], op0=ALU.mult, op1=ALU.add)
                    me.done(v.tensor_scalar(wp[:, p, n:n + NC_], ps[:, 2 * p + 1, 0:NC_], 0.125, None, ALU.mult),
                            ("sc", u))
                    mine(S, "dve", v, None)
                    me.done(v.tensor_reduce(sst[:, p, 0:1], wp[:, p, 0:n + NC_], AXX, ALU.max), ("mx", u))
                    mine(S, "dve", v, None)
                    me.done(v.tensor_tensor(sst[:, p, 0:1], sst[:, p, 0:1], sinkc[:, hh:hh + 1], ALU.max), ("ms", u))
                    mine(S, "dve", v, None)
                    me.done(v.tensor_scalar(sst[:, p, 1:2], sst[:, p, 0:1], -1.0, None, ALU.mult), ("nm", u))
                if u:
                    hh, b = UN[u - 1]
                    p = (u - 1) % 2
                    S["pe"].wait(v, ("O", u - 1))
                    me.done(v.tensor_copy(wo_[pr(hh), hh // 2, NC_ + b * P:NC_ + (b + 1) * P],
                                          ps[pr(hh), 5 + 2 * p, 256:384]), ("o", u - 1))
            for q in range(2):
                for m in range(KT):
                    add_gated(v, t + 18 + 8 * q + m, 3, 2, m, ctxt=False)
            end_of_updates(v, t + 33)
            v.memset(scr[:, 1:2], 0.0).then_inc(resid_ready, 1)

        def swa_pool(pool):
            h_wait(pool, "nm3")
            for dst, src in ((rtab, a["rtab"]), (rotm, a["rotm"])):
                pool.dma_start(dst, src).then_inc(swin, 16)

        SWA = (swa_pe, swa_act, swa_dve, swa_pool) if "swa" in MIX else None
        def sp_head(sp):
            for dst, src in const_loads:
                sp.dma_start(dst, src).then_inc(const_in, 16)
            sp.dma_start(tokbuf[:, :, :], a["tok1"].rearrange("(c p) n -> p c n", p=P)).then_inc(tok_in, 16)
            for n in range(16):
                ada_slab(sp, 0, n)

        def ada_slab(sp, L, n):
            g = 16 * L + n
            if g == 0:
                pass
            if n == 0 and L:
                h_wait(sp, f"nf{L - 1}")
            if g >= 2:
                sp.wait_ge(ada_prod, g - 1)
            v = ada_src[L].rearrange("(k p) n -> p k n", p=P)
            sp.dma_start(adaw[:, g % 2, :, :], v[:, :, n * AW:(n + 1) * AW]).then_inc(ada_landed2[g % 2], 16)

        def sp_tail(sp):
            for c in range(4):
                sp.wait_ge(out_ready, 2 * c + 2)
                sp.dma_start(out[c * P:(c + 1) * P, :], ostage[:, c, :]).then_inc(out_done, 16)
            sp.wait_ge(out_done, 64)

        out_ready = sem("out_ready")
        fin_tr = sem("fin_tr")

        def pe_main(pe):
            load_pe(pe, NCH, 0)
            pe.wait_ge(tr_copied, 16)
            with pe.Fori(0, 8) as i:
                for b in range(2):
                    ada_pe(pe, 0, i, b)
            for L in range(4):
                ctxt = L in (0, 2)
                if L == 2:
                    load_pe(pe, CCH, 16)
                norm_pe(pe, f"nm{L}")
                if MIXERS[L]:
                    MIXERS[L][0](pe)
                norm_pe(pe, f"nf{L}", ctxt)
                ffn_pe(pe, L, ctxt)
            norm_pe(pe, "nfin", False)
            h_wait(pe, "nfin")
            for c in range(4):
                for g in range(2):
                    n = 2 * c + g
                    if n >= 4:
                        pe.wait_ge(out_ready, n - 3)
                    for q in range(4):
                        mm = pe.transpose(ps[:, n % 4, q * P:(q + 1) * P],
                                          h[:, 4 * g + q, NC_ + c * P:NC_ + (c + 1) * P], ident[:, :])
                    mm.then_inc(fin_tr, 1)

        def act_main(act):
            act.wait_ge(const_in, 16 * CONSTS)
            act.activation(csil[:, :, :, :], csil[:, :, :, :], ACT.Silu).then_inc(csil_ready, 1)
            for L in range(4):
                ctxt = L in (0, 2)
                norm_act(act, f"nm{L}")
                if MIXERS[L]:
                    MIXERS[L][1](act)
                norm_act(act, f"nf{L}", ctxt)
                ffn_act(act, L, ctxt)
            norm_act(act, "nfin", False)

        def dve_main(dve):
            dve.wait_ge(const_in, 16 * CONSTS)
            load_dve(dve, NCH, 0)
            dve.wait_ge(tr_copied, 16)
            dve.memset(scr[:, 1:2], 0.0).then_inc(resid_ready, 1)
            with dve.Fori(0, 8) as i:
                for b in range(2):
                    ada_dve(dve, 0, i, b)
            for L in range(4):
                ctxt = L in (0, 2)
                if L == 2:
                    load_dve(dve, CCH, 16)
                    dve.wait_ge(tr_copied, 24)
                    dve.memset(scr[:, 1:2], 0.0).then_inc(resid_ready, 1)
                norm_dve_(dve, f"nm{L}", L, 2 * L, 0)
                if MIXERS[L]:
                    MIXERS[L][2](dve)
                else:
                    dve.memset(scr[:, 1:2], 0.0).then_inc(resid_ready, 1)
                norm_dve_(dve, f"nf{L}", L, 2 * L + 1, 3, ctxt)
                ffn_dve(dve, L, ctxt)
            norm_dve_(dve, "nfin", None, 8, 0, False)
            for n in range(8):
                dve.wait_ge(fin_tr, n + 1)
                dve.tensor_copy(ostage[:, n // 2, (n % 2) * 512:(n % 2 + 1) * 512], ps[:, n % 4, :])\
                    .then_inc(out_ready, 1)

        def pool_main(pool):
            for L in range(4):
                if L == 2:
                    pool.wait_ge(resid_ready, 5)
                    pool.dma_start(tokbuf[:, 0:CCH, :], a["tok2"].rearrange("(c p) n -> p c n", p=P))\
                        .then_inc(tok2_in, 16)
                if MIXERS[L]:
                    MIXERS[L][3](pool)
                ffn_pool(pool, L, L in (0, 2))

        flat = lambda v: v
        const_loads = [(csil[:, :, :, :], a["cvec"]), (adab[:, :, :], a["adab"]), (gains[:, :, :], a["gains"]),
                       (ident[:, :], a["ident"]), (ones[:, :], a["ones"]), (epsc[:, :], a["eps"]),
                       (maskL[:, :, :, :], a["maskL"]), (negm[:, :, :], a["negm"]), (tri[:, :, :], a["tri"]),
                       (convw[:, :, :], a["convw"]), (dng[:, :], a["dng"]), (gb2[:, :, :], a["gb2"]), (gng[:, :], a["gng"]), (mgb[:, :], a["mgb"]), (mhn[:, :], a["mhn"]), (sinkc[:, :], a["sink"])]
        CONSTS = len(const_loads)
        MIXERS = [(delta_pe, delta_act, delta_dve, delta_pool) if "dn" in MIX else None,
                  GLA, ML, SWA]

        block = ctx.enter_context(nc.Block())

        @block.sync
        def _(sp):
            sp_head(sp)
            down0 = {at[f"ffn{L}"][0] + 2 * n + 1: (L + 1, n) for L in range(3) for n in range(FFN_STEPS)}
            for s, (parts, _) in enumerate(slabs):
                if s in down0:
                    L, n = down0[s]
                    ada_slab(sp, L, 2 * n)
                    ada_slab(sp, L, 2 * n + 1)
                if s >= 2:
                    sp.wait_ge(tile_ready, slabs[s - 2][1] + 1)
                for off, kt, n, src in parts:
                    if off < 0:
                        dst = wslab(s, KT, 512)[:, :, 256 * (-off - 1):256 * -off]
                    else:
                        dst = wring[:, s % 2, off:off + kt * n].rearrange("p (k n) -> p k n", k=kt)
                    sp.dma_start(dst, src).then_inc(landed[s % 2], 16)
            sp_tail(sp)

        @block.tensor
        def _(pe):
            pe.sem_inc(tile_ready, 2)
            pe.sem_inc(pair_free[0], 1)
            pe.sem_inc(pair_free[1], 1)
            pe_main(pe)

        @block.scalar
        def _(act):
            act_main(act)

        @block.vector
        def _(dve):
            dve.sem_inc(ada_done, 1)
            dve_main(dve)

        @block.gpsimd
        def _(pool):
            pool.sem_inc(sqr_done, 1)
            pool_main(pool)


def kernel(**inputs):
    import concourse.bacc as _bacc
    from concourse.bass_utils import run_bass_kernel_spmd as _run

    x = {k: np.asarray(v) for k, v in inputs.items()}

    def cols(v):
        v = v.reshape(v.shape[:-1] + (v.shape[-1] // P, P))
        return np.moveaxis(v, -1, 0)

    f = np.float32
    jj, ii = np.arange(P)[:, None], np.arange(P)[None, :]
    lev = np.zeros((P, 2, LV, P), f)
    for l in range(LV):
        s = 1 << l
        m = (jj // (2 * s) == ii // (2 * s)) & (jj % (2 * s) < s) & (ii % (2 * s) >= s)
        lev[:, 0, l], lev[:, 1, l] = m, m.T
    tri = np.stack([(jj <= ii), (jj >= ii)], 1).astype(f)
    pos, inv = np.arange(NX), (10000.0 ** (-np.arange(16, dtype=f) / f(16))).astype(f)
    ang = np.concatenate([np.outer(inv, (pos // 64).astype(f)), np.outer(inv, (pos % 64).astype(f))], 0)
    rope = np.stack([np.tile(np.cos(ang), (4, 1)), np.tile(np.sin(ang), (4, 1))], 1).astype(f)
    rot = np.zeros((P, P), f)
    for m in range(P):
        rot[m + 32 if m % 64 < 32 else m - 32, m] = -1.0 if m % 64 < 32 else 1.0
    arrays = {
        "tok1": np.concatenate([x["ctx"][0], x["x"][0]], 0), "tok2": x["ctx_2"][0],
        "cvec": np.stack([np.stack([cols(x["c"][0]), cols(x["c_ctx"])], -1),
                          np.stack([cols(x["c_2"][0]), cols(x["c_ctx_2"])], -1)], 1),
        "adab": cols(np.concatenate([x["ada_b"], x["ada_b_2"]], 0)),
        "gains": cols(np.stack([x["norm_mix_g"][0], x["norm_ffn_g"][0], x["norm_mix_g"][1], x["norm_ffn_g"][1],
                                x["norm_mix_2"][0], x["norm_ffn_2"][0], x["norm_mix_2"][1], x["norm_ffn_2"][1],
                                x["final_norm_2"]], 0)),
        "ident": np.eye(P, dtype=f), "ones": np.ones((P, P), f), "eps": np.full((P, 1), EPS, f),
        "maskL": lev, "negm": (NEG * (1 - tri)).astype(f), "tri": tri,
        "convw": x["dn_conv_w"][0].reshape(32, P, 5).transpose(1, 0, 2), "dng": x["dn_norm_g"][0].reshape(P, 1),
        "dal": x["dn_a_log"].reshape(1, 32), "ddt": x["dn_dt_bias"].reshape(1, 32),
        "rst": np.broadcast_to((np.arange(T) % P != 0).astype(f), (P, T)),
        "gb2": cols(x["gla_gate_b2"][0]), "gng": cols(x["gla_norm_g"][0]),
        "gw2": x["gla_gate_w2"][0].transpose(1, 0, 2),
        "mgb": x["mlstm_gate_b_2"][0].reshape(32, 1), "mhn": cols(x["mlstm_head_norm_2"][0]),
        "sink": np.broadcast_to(x["swa_sink_2"], (P, 16)), "rtab": rope, "rotm": rot,
        "swa_k2": np.repeat(x["swa_w_in_2"][0][:, 1024:1280].reshape(D, 4, 1, 64), 2, 2).reshape(D, 512),
    }
    for k in ("ada_w", "ada_w_2", "ffn_w1", "ffn_w2", "ffn_w1_2", "ffn_w2_2"):
        arrays[k] = x[k]
    for k in ("dn_w_in", "dn_w_out", "gla_w_in", "gla_w_out", "mlstm_w_in_2", "mlstm_w_out_2", "swa_w_in_2",
              "swa_w_out_2"):
        arrays[k.removesuffix("_2")] = x[k][0]
    nc = _bacc.Bacc("TRN2", target_bir_lowering=False, num_devices=1)
    feed, aps = {}, {}
    for k, v in arrays.items():
        v = np.ascontiguousarray(v)
        feed[f"in_{k}"] = v
        aps[k] = nc.dram_tensor(f"in_{k}", v.shape, mybir.dt.from_np(v.dtype), kind="ExternalInput").ap()
    out = nc.dram_tensor("out", (NX, D), F32, kind="ExternalOutput").ap()
    build(nc, aps, out)
    r = _run(nc, [feed], core_ids=[0])
    return r.results[0]["out"].reshape(1, NX, D)
```
